# Optimizing a Trainium2 kernel written in Bass

```python
import jax, jax.numpy as jnp
from jax import lax
import numpy as np

D_MODEL = 1024
BATCH = 1
SEQ = 256
DEPTH = 2

N_MIXERS = 3
D_FF = 2816
EPS = 1e-6
CONV_WIDTH = 31
GLA_HEADS = 4
GLA_DK = D_MODEL // 2
GLA_DV = D_MODEL
GLA_HK = GLA_DK // GLA_HEADS
GLA_HV = GLA_DV // GLA_HEADS
GLA_GATE_RANK = 16
GLA_TAU = 16.0
GLA_CHUNK = 64
MOBA_HEADS = 8
MOBA_HEAD_DIM = D_MODEL // MOBA_HEADS
MOBA_BLOCK = 256
MOBA_TOPK = 3
MOBA_QCHUNK = 32

N_CONV = len(range(0, DEPTH, N_MIXERS))
N_GLA = len(range(1, DEPTH, N_MIXERS))
N_MOBA = len(range(2, DEPTH, N_MIXERS))

kernel_name = "hybrid_conv_gla_moba_macaron"

def rmsnorm(x, g):
    xf = x.astype(jnp.float32)
    y = xf * lax.rsqrt(jnp.mean(xf * xf, axis=-1, keepdims=True) + EPS)
    return (y * g.astype(jnp.float32)).astype(x.dtype)

def layernorm(x, g, b):
    xf = x.astype(jnp.float32)
    mu = jnp.mean(xf, axis=-1, keepdims=True)
    var = jnp.mean(jnp.square(xf - mu), axis=-1, keepdims=True)
    y = (xf - mu) * lax.rsqrt(var + EPS) * g.astype(jnp.float32) + b.astype(jnp.float32)
    return y.astype(x.dtype)

def swiglu(x, w_gate, w_up, w_down):
    return (jax.nn.silu(x @ w_gate) * (x @ w_up)) @ w_down

def conformer_conv(x, w_pw1, b_pw1, w_dw, b_dw, ln_g, ln_b, w_pw2, b_pw2):
    a, gt = jnp.split(x @ w_pw1 + b_pw1, 2, axis=-1)
    h = a * jax.nn.sigmoid(gt)
    h = lax.conv_general_dilated(
        h, w_dw[:, None, :].astype(h.dtype), window_strides=(1,),
        padding=[(CONV_WIDTH - 1, 0)],
        dimension_numbers=("NWC", "WIO", "NWC"),
        feature_group_count=D_MODEL) + b_dw
    h = jax.nn.silu(layernorm(h, ln_g, ln_b))
    return h @ w_pw2 + b_pw2

def gla_mixer(x, w_q, w_k, w_v, w_a1, w_a2, b_a, w_r, b_r, norm_g, w_o):
    B, S, _ = x.shape
    nc = S // GLA_CHUNK
    f32 = jnp.float32

    def heads(t, hd):
        return t.reshape(B, nc, GLA_CHUNK, GLA_HEADS, hd).transpose(1, 0, 3, 2, 4)

    q = heads((x @ w_q).astype(f32) * GLA_HK ** -0.5, GLA_HK)
    k = heads((x @ w_k).astype(f32), GLA_HK)
    v = heads((x @ w_v).astype(f32), GLA_HV)
    log_a = heads(jax.nn.log_sigmoid(((x @ w_a1) @ w_a2 + b_a).astype(f32)) / GLA_TAU, GLA_HK)
    causal = jnp.tril(jnp.ones((GLA_CHUNK, GLA_CHUNK), dtype=bool))

    def step(state, inp):
        qc, kc, vc, lac = inp
        b = jnp.cumsum(lac, axis=2)
        diff = b[:, :, :, None, :] - b[:, :, None, :, :]
        decay = jnp.exp(jnp.where(causal[:, :, None], diff, -jnp.inf))
        att = jnp.einsum("bhtd,bhsd,bhtsd->bhts", qc, kc, decay)
        o = att @ vc + jnp.einsum("bhtd,bhdv->bhtv", qc * jnp.exp(b), state)
        b_last = b[:, :, -1:, :]
        state = (jnp.exp(b_last[:, :, 0, :, None]) * state
                 + jnp.einsum("bhsd,bhsv->bhdv", kc * jnp.exp(b_last - b), vc))
        return state, o

    s0 = jnp.zeros((B, GLA_HEADS, GLA_HK, GLA_HV), f32)
    _, o = lax.scan(step, s0, (q, k, v, log_a))
    o = o.transpose(1, 0, 3, 2, 4).reshape(B, S, GLA_HEADS, GLA_HV)
    o = rmsnorm(o, norm_g).reshape(B, S, GLA_DV).astype(x.dtype)
    r = jax.nn.silu(x @ w_r + b_r)
    return (o * r) @ w_o

def moba_mixer(x, w_q, w_k, w_v, w_o):
    B, S, _ = x.shape
    H, Dh, L, Cq = MOBA_HEADS, MOBA_HEAD_DIM, MOBA_BLOCK, MOBA_QCHUNK
    f32 = jnp.float32
    nb = -(-S // L)
    sp = nb * L
    nq = S // Cq
    slopes = 2.0 ** (-8.0 * jnp.arange(1, H + 1, dtype=f32) / H)

    def heads(t):
        return t.reshape(B, S, H, Dh).transpose(0, 2, 1, 3).astype(f32)

    q = heads(x @ w_q) * Dh ** -0.5
    k = heads(x @ w_k)
    v = heads(x @ w_v)
    pad = ((0, 0), (0, 0), (0, sp - S), (0, 0))
    kb = jnp.pad(k, pad).reshape(B, H, nb, L, Dh)
    vb = jnp.pad(v, pad).reshape(B, H, nb, L, Dh)

    pos = jnp.arange(S)
    q_blk = pos // L
    k_mean = jnp.mean(kb, axis=3)
    gate = jnp.einsum("bhsd,bhnd->bhsn", q, k_mean)
    gate = jnp.where(jnp.arange(nb)[None, :] < q_blk[:, None], gate, -jnp.inf)
    k_sel = min(MOBA_TOPK, nb)
    _, sel = lax.top_k(gate, k_sel)
    valid = sel < q_blk[:, None]

    def chunks(t):
        return jnp.moveaxis(t.reshape(B, H, nq, Cq, *t.shape[3:]), 2, 0)

    bi = jnp.arange(B)[:, None, None, None]
    hi = jnp.arange(H)[None, :, None, None]

    def attend(inp):
        qc, selc, validc, c = inp
        tq = c * Cq + jnp.arange(Cq)
        own = (c * Cq) // L
        k_own = lax.dynamic_index_in_dim(kb, own, axis=2, keepdims=False)
        v_own = lax.dynamic_index_in_dim(vb, own, axis=2, keepdims=False)
        kg = kb[bi, hi, selc]
        vg = vb[bi, hi, selc]
        dist_own = (tq[:, None] - (own * L + jnp.arange(L))[None, :]).astype(f32)
        sc_own = jnp.einsum("bhqd,bhsd->bhqs", qc, k_own) - slopes[:, None, None] * dist_own
        sc_own = jnp.where(dist_own >= 0, sc_own, -jnp.inf)
        past_pos = selc[..., None] * L + jnp.arange(L)
        dist_past = (tq[:, None, None] - past_pos).astype(f32)
        sc_past = (jnp.einsum("bhqd,bhqjsd->bhqjs", qc, kg)
                   - slopes[:, None, None, None] * dist_past)
        sc_past = jnp.where(validc[..., None], sc_past, -jnp.inf)
        scores = jnp.concatenate([sc_own, sc_past.reshape(B, H, Cq, k_sel * L)], axis=-1)
        p = jax.nn.softmax(scores, axis=-1)
        out = (jnp.einsum("bhqs,bhsd->bhqd", p[..., :L], v_own)
               + jnp.einsum("bhqjs,bhqjsd->bhqd",
                            p[..., L:].reshape(B, H, Cq, k_sel, L), vg))
        return out

    o = lax.map(attend, (chunks(q), chunks(sel), chunks(valid), jnp.arange(nq)))
    o = o.transpose(1, 0, 3, 2, 4).reshape(B, S, H * Dh).astype(x.dtype)
    return o @ w_o

def setup_inputs(seed: int = 0) -> dict:
    key = jax.random.key(seed)
    ks = iter(jax.random.split(key, 64))
    f32 = jnp.float32

    def w(shape, fan_in):
        return jax.random.normal(next(ks), shape, f32) * fan_in ** -0.5

    def gain(shape):
        return 1.0 + 0.05 * jax.random.normal(next(ks), shape, f32)

    def bias(shape, scale=0.02):
        return scale * jax.random.normal(next(ks), shape, f32)

    D, F = D_MODEL, D_FF
    return {
        "x": jax.random.normal(next(ks), (BATCH, SEQ, D), f32),
        "g_ffn1": gain((DEPTH, D)),
        "g_mix": gain((DEPTH, D)),
        "g_ffn2": gain((DEPTH, D)),
        "g_final": gain((D,)),
        "w1_gate": w((DEPTH, D, F), D),
        "w1_up": w((DEPTH, D, F), D),
        "w1_down": w((DEPTH, F, D), F),
        "w2_gate": w((DEPTH, D, F), D),
        "w2_up": w((DEPTH, D, F), D),
        "w2_down": w((DEPTH, F, D), F),
        "cv_w_pw1": w((N_CONV, D, 2 * D), D),
        "cv_b_pw1": bias((N_CONV, 2 * D)),
        "cv_w_dw": w((N_CONV, CONV_WIDTH, D), CONV_WIDTH),
        "cv_b_dw": bias((N_CONV, D)),
        "cv_ln_g": gain((N_CONV, D)),
        "cv_ln_b": bias((N_CONV, D)),
        "cv_w_pw2": w((N_CONV, D, D), D),
        "cv_b_pw2": bias((N_CONV, D)),
        "gla_w_q": w((N_GLA, D, GLA_DK), D),
        "gla_w_k": w((N_GLA, D, GLA_DK), D),
        "gla_w_v": w((N_GLA, D, GLA_DV), D),
        "gla_w_a1": w((N_GLA, D, GLA_GATE_RANK), D),
        "gla_w_a2": w((N_GLA, GLA_GATE_RANK, GLA_DK), GLA_GATE_RANK),
        "gla_b_a": bias((N_GLA, GLA_DK), 0.1),
        "gla_w_r": w((N_GLA, D, GLA_DV), D),
        "gla_b_r": bias((N_GLA, GLA_DV)),
        "gla_norm_g": gain((N_GLA, GLA_HV)),
        "gla_w_o": w((N_GLA, GLA_DV, D), GLA_DV),
        "mb_w_q": w((N_MOBA, D, MOBA_HEADS * MOBA_HEAD_DIM), D),
        "mb_w_k": w((N_MOBA, D, MOBA_HEADS * MOBA_HEAD_DIM), D),
        "mb_w_v": w((N_MOBA, D, MOBA_HEADS * MOBA_HEAD_DIM), D),
        "mb_w_o": w((N_MOBA, MOBA_HEADS * MOBA_HEAD_DIM, D), MOBA_HEADS * MOBA_HEAD_DIM),
    }

def reference(x, g_ffn1, g_mix, g_ffn2, g_final,
              w1_gate, w1_up, w1_down, w2_gate, w2_up, w2_down,
              cv_w_pw1, cv_b_pw1, cv_w_dw, cv_b_dw, cv_ln_g, cv_ln_b, cv_w_pw2, cv_b_pw2,
              gla_w_q, gla_w_k, gla_w_v, gla_w_a1, gla_w_a2, gla_b_a, gla_w_r, gla_b_r,
              gla_norm_g, gla_w_o,
              mb_w_q, mb_w_k, mb_w_v, mb_w_o):
    h = x
    for i in range(DEPTH):
        h = h + 0.5 * swiglu(rmsnorm(h, g_ffn1[i]), w1_gate[i], w1_up[i], w1_down[i])
        u = rmsnorm(h, g_mix[i])
        kind = i % N_MIXERS
        j = i // N_MIXERS
        if kind == 0:
            m = conformer_conv(u, cv_w_pw1[j], cv_b_pw1[j], cv_w_dw[j], cv_b_dw[j],
                               cv_ln_g[j], cv_ln_b[j], cv_w_pw2[j], cv_b_pw2[j])
        elif kind == 1:
            m = gla_mixer(u, gla_w_q[j], gla_w_k[j], gla_w_v[j], gla_w_a1[j], gla_w_a2[j],
                          gla_b_a[j], gla_w_r[j], gla_b_r[j], gla_norm_g[j], gla_w_o[j])
        else:
            m = moba_mixer(u, mb_w_q[j], mb_w_k[j], mb_w_v[j], mb_w_o[j])
        h = h + m
        h = h + 0.5 * swiglu(rmsnorm(h, g_ffn2[i]), w2_gate[i], w2_up[i], w2_down[i])
    return rmsnorm(h, g_final)


_drawn_inputs = setup_inputs


def setup_inputs(seed=0):
    import zlib

    import numpy as np

    out = dict(_drawn_inputs(seed))
    spreads = {}
    factors = {'cv_ln_b': 3.987, 'gla_b_a': 3.074, 'gla_b_r': 6.302, 'cv_b_pw1': 3.588}
    for name, (base, spread) in spreads.items():
        noise = np.random.default_rng([zlib.crc32(name.encode()), seed]).standard_normal(out[name].shape)
        drawn = base * np.exp(spread * noise) if base else spread * noise
        out[name] = __import__('jax').numpy.asarray(drawn.astype(out[name].dtype))
    for name, factor in factors.items():
        out[name] = (out[name] * factor).astype(out[name].dtype)
    return out
```

```python
from contextlib import ExitStack

import numpy as np

import concourse.bass as bass
from concourse import mybir
from concourse.alu_op_type import AluOpType as ALU

F32 = mybir.dt.float32
F32R = mybir.dt.float32r
ACT = mybir.ActivationFunctionType
AX_X = mybir.AxisListType.X

P = 128
D = 1024
SEQ = 256
FF = 2816
TOKS = SEQ // P
KT = D // P
EPS = 1e-6
UNIT = 2048
SLOTS = 3
CHUNKS = FF // 256
FFN_UNITS = 3 * CHUNKS
TAPS = 31
PAD = TAPS - 1
CV_CHUNKS = D // 256
CV_UNITS = 2 * CV_CHUNKS + 4
HEADS = 4
HK = 128
HV = 256
TAU = 16.0
LEVELS = 8
GLA_UNITS = 16

U_FFN = [0, FFN_UNITS + CV_UNITS, 2 * FFN_UNITS + CV_UNITS, 3 * FFN_UNITS + CV_UNITS + GLA_UNITS]
U_CONV = FFN_UNITS
U_GLA = 3 * FFN_UNITS + CV_UNITS
UNITS = U_FFN[3] + FFN_UNITS
PHASE_OF_FFN = [0, 2, 3, 5]

DW_DVE = 6
DW_PE = KT - DW_DVE

C_NORM = 0
C_DW = C_NORM + 6 * KT
C_BDW = C_DW + KT * TAPS
C_LNG = C_BDW + KT
C_LNB = C_LNG + KT
C_BA = C_LNB + KT
C_END = C_BA + HEADS
R_BPW1 = 0
R_BPW2 = R_BPW1 + 2 * D
R_BR = R_BPW2 + D
R_NG = R_BR + D
R_GF = R_NG + HV
R_END = R_GF + D
SCORES = LEVELS * P



def build(nc, stream, x, chan, rows, a1, a2, masks, ident_d, out):
    with ExitStack() as ctx:
        def sb(name, shape, dt=F32):
            return ctx.enter_context(nc.sbuf_tensor(name, shape, dt))

        def sem(name):
            return ctx.enter_context(nc.semaphore(name))

        ps = ctx.enter_context(nc.psum_tensor("ps", [P, 8, 512], F32))
        GU, DN, TR = 0, 2, 6

        h = sb("h", [P, TOKS, D])
        raw = sb("raw", [P, SLOTS, UNIT])
        whi = sb("whi", [P, SLOTS, UNIT], F32R)
        wlo = sb("wlo", [P, SLOTS, UNIT], F32R)
        xhi = sb("xhi", [P, KT, SEQ], F32R)
        xlo = sb("xlo", [P, KT, SEQ], F32R)
        ghi = sb("ghi", [P, 2, SEQ], F32R)
        glo = sb("glo", [P, 2, SEQ], F32R)
        pair = sb("pair", [P, D])
        silu_g = pair[:, 0:512].rearrange("p (t c) -> p t c", t=TOKS)
        gated = pair[:, 512:1024].rearrange("p (t c) -> p t c", t=TOKS)
        squares = sb("squares", [P, D])
        chan_sb = sb("chan_sb", [P, C_END])
        rows_sb = sb("rows_sb", [P, R_GF - R_BR])
        ident = sb("ident", [P, P])
        mask_sb = sb("mask_sb", [P, LEVELS, P])
        a1_raw = sb("a1_raw", [P, KT * 16])
        a1_hi = sb("a1_hi", [P, KT * 16], F32R)
        a1_lo = sb("a1_lo", [P, KT * 16], F32R)
        a2_sb = sb("a2_sb", [16, HEADS * HK])
        mean_w = sb("mean_w", [P, P])
        sumsq = sb("sumsq", [P, TOKS])
        ms = sb("ms", [P, TOKS])
        rstd = sb("rstd", [P, TOKS])
        neg_half = sb("neg_half", [P, TOKS * HEADS])
        eps_sb = sb("eps_sb", [P, 1])
        WORK = 20288
        work = sb("work", [P, WORK])

        def area(at, *shape):
            n = int(np.prod(shape))
            v = work[:, at:at + n]
            assert at + n <= WORK, (at, n)
            if len(shape) == 2:
                v = v.rearrange("p (a b) -> p a b", a=shape[0])
            if len(shape) == 3:
                v = v.rearrange("p (a b c) -> p a b c", a=shape[0], b=shape[1])
            return v, at + n

        diag, at = area(0, DW_PE, TAPS, P)
        hb, at = area(at, KT, PAD + SEQ)
        cvo, at = area(at, KT, SEQ)
        cvs, at = area(at, KT, SEQ)
        ag, at = area(at, TOKS, 512)
        sg, at = area(at, TOKS, 256)
        ln_std, at = area(at, SEQ)
        ln_rstd, at = area(at, SEQ)
        cvb, at = area(at, R_BR)
        q_tok = squares[:, :].rearrange("p (t c) -> p t c", t=TOKS)
        k_tok = pair[:, :].rearrange("p (t c) -> p t c", t=TOKS)
        qT, at = area(0, HEADS, SEQ)
        kT, at = area(at, HEADS, SEQ)
        v_sb, at = area(at, TOKS, D)
        rg, at = area(at, TOKS, D)
        y_at = at
        zb, at = area(at, HEADS, SEQ)
        dif0, at = area(at, HEADS, SEQ)
        dif1, at = area(at, HEADS, SEQ)
        b64, at = area(at, HEADS, SEQ)
        b256, at = area(at, HEADS, SEQ)
        qk, at = area(at, LEVELS, HEADS * SEQ)
        keep64, at = area(at, SEQ)
        keep_all, at = area(at, SEQ)
        za, at = area(at, TOKS, 16)
        aT, at = area(at, SEQ)
        o_ss, at = area(at, 8)
        o_ms, at = area(at, 8)
        o_rstd, at = area(at, 8)
        dif = [dif0, dif1]
        masked = [squares[:, :].rearrange("p (l t) -> p l t", l=LEVELS),
                  pair[:, :].rearrange("p (l t) -> p l t", l=LEVELS)]
        y_tok, at2 = area(y_at, TOKS, D)
        attn, at2 = area(at2, HEADS * 3, P)

        loaded = sem("loaded")
        bias_loaded = sem("bias_loaded")
        gain_loaded = sem("gain_loaded")
        raw_landed = [sem(f"raw_landed{s}") for s in range(SLOTS)]
        hi_made = sem("hi_made")
        lo_made = sem("lo_made")
        unit_used = sem("unit_used")
        h_added = sem("h_added")
        x_trans = sem("x_trans")
        x_hi = sem("x_hi")
        x_lo = sem("x_lo")
        squares_done = sem("squares_done")
        ms_done = sem("ms_done")
        rstd_ready = sem("rstd_ready")
        silu_done = sem("silu_done")
        gated_done = sem("gated_done")
        g_trans = sem("g_trans")
        g_hi = sem("g_hi")
        g_lo = sem("g_lo")
        down_half = sem("down_half")
        const_made = sem("const_made")
        diag_made = sem("diag_made")
        cv_bias = sem("cv_bias")
        cv_sig = sem("cv_sig")
        cv_gated = sem("cv_gated")
        cv_trans = sem("cv_trans")
        hb_zero = sem("hb_zero")
        hb_ready = sem("hb_ready")
        dw_step = sem("dw_step")
        dw_pe = sem("dw_pe")
        dw_out = sem("dw_out")
        mean_done = sem("mean_done")
        centred = sem("centred")
        cv_squares = sem("cv_squares")
        var_done = sem("var_done")
        std_done = sem("std_done")
        ln_rstd_done = sem("ln_rstd_done")
        normed = sem("normed")
        cv_act = sem("cv_act")
        z_hi = sem("z_hi")
        z_lo = sem("z_lo")
        bias_added = sem("bias_added")
        a1_split = sem("a1_split")
        za_done = sem("za_done")
        za_scaled = sem("za_scaled")
        za_trans = sem("za_trans")
        aT_ready = sem("aT_ready")
        a2_done = sem("a2_done")
        zb_ready = sem("zb_ready")
        soft = sem("soft")
        la_ready = sem("la_ready")
        scanned = sem("scanned")
        keep_ready = sem("keep_ready")
        qk_tok = sem("qk_tok")
        v_ready = sem("v_ready")
        r_biased = sem("r_biased")
        r_silu = sem("r_silu")
        rg_ready = sem("rg_ready")
        qk_trans = sem("qk_trans")
        qkT_ready = sem("qkT_ready")
        dif_ready = sem("dif_ready")
        decay_ready = sem("decay_ready")
        qk_ready = sem("qk_ready")
        scores = sem("scores")
        masked_ready = sem("masked_ready")
        fold_a = sem("fold_a")
        fold_b = sem("fold_b")
        attn_ready = sem("attn_ready")
        o_done = sem("o_done")
        o_squares = sem("o_squares")
        o_ms_done = sem("o_ms_done")
        o_rstd_done = sem("o_rstd_done")
        y_ready = sem("y_ready")
        y_trans = sem("y_trans")
        y_hi = sem("y_hi")
        y_lo = sem("y_lo")
        out_ready = sem("out_ready")
        stored = sem("stored")

        LOADS = 16 * 6
        DW_LAST = (TAPS - 1) * DW_DVE

        block = ctx.enter_context(nc.Block())

        @block.sync
        def _(sp):
            sp.dma_start(h[:, :, :], x.rearrange("a (t p) d -> p (a t) d", p=P)).then_inc(loaded, 16)
            sp.dma_start(ident[:, :], ident_d).then_inc(loaded, 16)
            sp.dma_start(chan_sb[:, :], chan).then_inc(loaded, 16)
            for s in range(SLOTS):
                sp.dma_start(raw[:, s, :], stream[s, :, :]).then_inc(raw_landed[s], 16)
            sp.dma_start(cvb, rows[0:R_BR].partition_broadcast(P)).then_inc(bias_loaded, 16)
            sp.dma_start(rows_sb[:, :], rows[R_BR:R_GF].partition_broadcast(P)).then_inc(bias_loaded, 16)
            sp.dma_start(a1_raw[:, :], a1).then_inc(loaded, 16)
            sp.dma_start(a2_sb[:, :], a2).then_inc(loaded, 16)
            sp.dma_start(mask_sb[:, :, :].rearrange("p a b -> p (a b)"), masks).then_inc(loaded, 16)

            def load(u, slot):
                sp.wait_ge(lo_made, u - SLOTS + 1)
                sp.dma_start(raw[:, slot, :], stream[bass.ds(u, 1), :, :]
                             .rearrange("a p n -> p (a n)")).then_inc(raw_landed[slot], 16)

            whole = UNITS // SLOTS
            with sp.Fori(1, whole) as turn:
                for slot in range(SLOTS):
                    load(turn * SLOTS + slot, slot)
            for u in range(whole * SLOTS, UNITS):
                load(u, u % SLOTS)
            sp.wait_ge(g_trans, 4 * CHUNKS)
            sp.dma_start(pair[:, :], rows[R_GF:R_END].partition_broadcast(P)).then_inc(gain_loaded, 16)
            sp.wait_ge(out_ready, TOKS)
            sp.dma_start(out.rearrange("a (t p) d -> p (a t) d", p=P), h[:, :, :]).then_inc(stored, 16)
            sp.wait_ge(stored, 16)

        @block.tensor
        def _(pe):
            def unit_ready(u):
                pe.wait_ge(hi_made, u + 1)
                pe.wait_ge(lo_made, u + 1)

            def three(o, xh, xl, wh, wl, first, last):
                nc.tensor.matmul(o, xh, wh, start=first, stop=False)
                nc.tensor.matmul(o, xh, wl, start=False, stop=False)
                return nc.tensor.matmul(o, xl, wh, start=False, stop=last)

            def wide_unit(u, slot, half, bank, phase=None):
                unit_ready(u)
                for k in range(4):
                    kt = 4 * half + k
                    if phase is not None:
                        pe.wait_ge(x_hi, KT * phase + kt + 1)
                        pe.wait_ge(x_lo, KT * phase + kt + 1)
                    w = slice(k * 512, k * 512 + 512)
                    for t in range(TOKS):
                        s = slice(t * P, t * P + P)
                        last = three(ps[:, bank + t, :], xhi[:, kt, s], xlo[:, kt, s],
                                     whi[:, slot, w], wlo[:, slot, w], kt == 0, kt == KT - 1)
                last.then_inc(unit_used, 1)

            def down_unit(u, slot, srch, srcl, k0, first, final):
                unit_ready(u)
                for half in range(2):
                    for t in range(TOKS):
                        s = slice(t * P, t * P + P)
                        for k in range(2):
                            w = slice(k * D + half * 512, k * D + half * 512 + 512)
                            last = three(ps[:, DN + 2 * t + half, :], srch[:, k0 + k, s], srcl[:, k0 + k, s],
                                         whi[:, slot, w], wlo[:, slot, w], first and k == 0, final and k == 1)
                    if final and half == 0:
                        last.then_inc(down_half, 1)
                last.then_inc(unit_used, 1)

            def turn(bank, src, c0):
                for k in range(2):
                    for t in range(TOKS):
                        last = nc.tensor.transpose(ps[:, bank, k * SEQ + t * P:k * SEQ + t * P + P],
                                                   src[:, t, c0 + k * P:c0 + k * P + P], ident[:, :])
                return last

            def norm_transposes(phase):
                for j in range(4):
                    if phase == 0:
                        if j == 0:
                            pe.wait_ge(loaded, LOADS)
                    else:
                        pe.wait_ge(h_added, 4 * (phase - 1) + 2 * (j // 2 + 1))
                    if j >= 2:
                        pe.wait_ge(x_hi, KT * phase + 2 * (j - 2) + 2)
                        pe.wait_ge(x_lo, KT * phase + 2 * (j - 2) + 2)
                    turn(TR + j % 2, h, 2 * j * P).then_inc(x_trans, 1)

            def ffn(f):
                phase, u0, s0 = PHASE_OF_FFN[f], U_FFN[f], U_FFN[f] % SLOTS
                g0 = f * CHUNKS

                def chunk(n, first):
                    u = u0 + 3 * n - 1
                    pe.wait_ge(gated_done, 2 * (g0 + n))
                    wide_unit(u, (s0 + 2) % SLOTS, 0, GU)
                    turn(TR, gated, 0).then_inc(g_trans, 1)
                    wide_unit(u + 1, s0, 1, GU)
                    pe.wait_ge(g_hi, g0 + n)
                    pe.wait_ge(g_lo, g0 + n)
                    down_unit(u + 2, (s0 + 1) % SLOTS, ghi, glo, 0, first, False)

                norm_transposes(phase)
                wide_unit(u0, s0, 0, GU, phase)
                wide_unit(u0 + 1, (s0 + 1) % SLOTS, 1, GU, phase)
                chunk(1, True)
                with pe.Fori(2, CHUNKS) as n:
                    chunk(n, False)
                pe.wait_ge(gated_done, 2 * (g0 + CHUNKS))
                turn(TR, gated, 0).then_inc(g_trans, 1)
                pe.wait_ge(g_hi, g0 + CHUNKS)
                pe.wait_ge(g_lo, g0 + CHUNKS)
                down_unit(u0 + FFN_UNITS - 1, (s0 + 2) % SLOTS, ghi, glo, 0, False, True)

            def conv():
                norm_transposes(1)
                for c in range(CV_CHUNKS):
                    u = U_CONV + 2 * c
                    bank = 2 * (c % 2)
                    if c >= 2:
                        pe.wait_ge(cv_bias, 2 * (c - 1))
                    wide_unit(u, u % SLOTS, 0, bank, 1 if c == 0 else None)
                    if c >= 1:
                        pe.wait_ge(cv_gated, 2 * c)
                        if c >= 3:
                            pe.wait_ge(hb_ready, c - 2)
                        turn(TR + (c - 1) % 2, gated, 0).then_inc(cv_trans, 1)
                    wide_unit(u + 1, (u + 1) % SLOTS, 1, bank, 1 if c == 0 else None)
                pe.wait_ge(cv_gated, 2 * CV_CHUNKS)
                pe.wait_ge(hb_ready, CV_CHUNKS - 2)
                turn(TR + (CV_CHUNKS - 1) % 2, gated, 0).then_inc(cv_trans, 1)
                pe.wait_ge(diag_made, DW_PE)
                pe.wait_ge(hb_ready, CV_CHUNKS)
                for i in range(DW_PE):
                    for j in range(TAPS):
                        last = nc.tensor.matmul(ps[:, 4 + i, 0:SEQ], diag[:, i, j, :],
                                                hb[:, DW_DVE + i, j:j + SEQ], start=(j == 0), stop=(j == TAPS - 1))
                    last.then_inc(dw_pe, 1)
                pe.wait_ge(const_made, 1)
                order = list(range(DW_DVE, KT)) + list(range(DW_DVE))
                for n, ct in enumerate(order):
                    if ct >= DW_DVE:
                        pe.wait_ge(dw_out, ct - DW_DVE + 1)
                    else:
                        pe.wait_ge(dw_step, DW_LAST + ct + 1)
                    last = nc.tensor.matmul(ps[:, 6, 0:SEQ], mean_w[:, :], cvo[:, ct, :],
                                            start=(n == 0), stop=(n == KT - 1))
                last.then_inc(mean_done, 1)
                for ct in range(KT):
                    if ct % 2 == 0:
                        pe.wait_ge(cv_squares, ct // 2 + 1)
                    last = nc.tensor.matmul(ps[:, 7, 0:SEQ], mean_w[:, :], cvs[:, ct, :],
                                            start=(ct == 0), stop=(ct == KT - 1))
                last.then_inc(var_done, 1)
                for k in range(4):
                    u = U_CONV + 2 * CV_CHUNKS + k
                    pe.wait_ge(z_hi, k + 1)
                    pe.wait_ge(z_lo, k + 1)
                    down_unit(u, u % SLOTS, xhi, xlo, 2 * k, k == 0, k == 3)

            def gla():
                norm_transposes(4)
                pe.wait_ge(a1_split, 2)
                pe.wait_ge(x_hi, KT * 5)
                pe.wait_ge(x_lo, KT * 5)
                for t in range(TOKS):
                    s = slice(t * P, t * P + P)
                    for kt in range(KT):
                        w = slice(kt * 16, kt * 16 + 16)
                        last = three(ps[:, 4, t * 16:t * 16 + 16], xhi[:, kt, s], xlo[:, kt, s],
                                     a1_hi[:, w], a1_lo[:, w], kt == 0, kt == KT - 1)
                last.then_inc(za_done, 1)

                def unit(k, bank):
                    u = U_GLA + k
                    wide_unit(u, u % SLOTS, k % 2, bank)

                unit(0, 0)
                unit(1, 0)
                pe.wait_ge(za_scaled, TOKS)
                for t in range(TOKS):
                    last = nc.tensor.transpose(ps[0:16, 5, t * P:t * P + P], za[:, t, :], ident[:, :])
                last.then_inc(za_trans, 1)
                unit(2, 2)
                pe.wait_ge(aT_ready, 1)
                for hd in range(HEADS):
                    last = nc.tensor.matmul(ps[:, 4 + hd // 2, (hd % 2) * SEQ:(hd % 2) * SEQ + SEQ],
                                            a2_sb[:, hd * HK:hd * HK + HK], aT[0:16, :], start=True, stop=True)
                last.then_inc(a2_done, 1)
                unit(3, 2)
                pe.wait_ge(qk_tok, 2)
                for b in range(2):
                    turn(TR + b, q_tok, b * 256).then_inc(qk_trans, 1)
                unit(4, 0)
                pe.wait_ge(qk_tok, 4)
                for b in range(2):
                    pe.wait_ge(qkT_ready, b + 1)
                    turn(TR + b, k_tok, b * 256).then_inc(qk_trans, 1)
                unit(5, 0)
                unit(6, 2)
                unit(7, 2)
                pe.wait_ge(r_biased, 2)
                unit(8, 0)
                unit(9, 0)
                pe.wait_ge(r_biased, 4)
                unit(10, 2)
                unit(11, 2)
                pe.wait_ge(qkT_ready, 4)
                pe.wait_ge(zb_ready, HEADS)
                for i in range(2 * HEADS):
                    hd, tile = i // 2, i % 2
                    bank = 4 + 2 * (i % 2)
                    if i >= 2:
                        pe.wait_ge(masked_ready, i - 1)
                    s = slice(tile * P, tile * P + P)
                    nc.tensor.matmul(ps[:, bank, 0:P], kT[:, hd, s], qT[:, hd, s], start=True, stop=True)
                    for lv in range(1, LEVELS):
                        if i == 0:
                            pe.wait_ge(qk_ready, 2 * lv)
                        both = qk[:, lv - 1, hd * SEQ + tile * P:hd * SEQ + tile * P + P]
                        last = nc.tensor.matmul(ps[:, bank + lv // 4, (lv % 4) * P:(lv % 4) * P + P],
                                                both, both, start=True, stop=True)
                    last.then_inc(scores, 1)
                pe.wait_ge(masked_ready, 2 * HEADS - 1)
                pe.wait_ge(qk_ready, 2 * LEVELS)
                for hd in range(HEADS):
                    last = nc.tensor.matmul(ps[:, 4, hd * P:hd * P + P],
                                            qk[:, LEVELS - 1, hd * SEQ:hd * SEQ + P],
                                            qk[:, LEVELS - 1, hd * SEQ + P:hd * SEQ + SEQ], start=True, stop=True)
                last.then_inc(scores, 1)
                pe.wait_ge(v_ready, 4)
                pe.wait_ge(attn_ready, 2 * HEADS + 1)
                for hd in range(HEADS):
                    c = slice((hd % 2) * HV, (hd % 2) * HV + HV)
                    vc = slice(hd * HV, hd * HV + HV)
                    nc.tensor.matmul(ps[:, hd // 2, c], attn[:, 3 * hd, :], v_sb[:, 0, vc], start=True, stop=True)
                    nc.tensor.matmul(ps[:, 2 + hd // 2, c], attn[:, 3 * hd + 2, :], v_sb[:, 0, vc],
                                     start=True, stop=False)
                    nc.tensor.matmul(ps[:, 2 + hd // 2, c], attn[:, 3 * hd + 1, :], v_sb[:, 1, vc],
                                     start=False, stop=True).then_inc(o_done, 1)
                for j in range(4):
                    pe.wait_ge(y_ready, 2 * (j + 1))
                    if j >= 2:
                        pe.wait_ge(y_hi, j - 1)
                        pe.wait_ge(y_lo, j - 1)
                    turn(TR + j % 2, y_tok, j * 256).then_inc(y_trans, 1)
                for k in range(4):
                    u = U_GLA + 12 + k
                    pe.wait_ge(y_hi, k + 1)
                    pe.wait_ge(y_lo, k + 1)
                    down_unit(u, u % SLOTS, xhi, xlo, 2 * k, k == 0, k == 3)

            ffn(0)
            conv()
            ffn(1)
            ffn(2)
            gla()
            ffn(3)

        @block.scalar
        def _(act):
            def convert(u):
                if u >= UNITS:
                    return
                slot = u % SLOTS
                if u >= SLOTS:
                    act.wait_ge(unit_used, u - SLOTS + 1)
                act.wait_ge(raw_landed[slot], 16 * (u // SLOTS + 1))
                nc.scalar.copy(whi[:, slot, :], raw[:, slot, :]).then_inc(hi_made, 1)

            def convert_in_loop(u0, n, k):
                slot = (u0 + k) % SLOTS
                act.wait_ge(unit_used, u0 + 3 * n + k - SLOTS + 1)
                act.wait_ge(raw_landed[slot], 16 * ((u0 + k) // SLOTS + 1) + 16 * n)
                nc.scalar.copy(whi[:, slot, :], raw[:, slot, :]).then_inc(hi_made, 1)

            def norm_in(phase):
                for kt in range(KT):
                    if kt % 2 == 0:
                        act.wait_ge(x_trans, 4 * phase + kt // 2 + 1)
                    nc.scalar.activation(xhi[:, kt, :], ps[:, TR + (kt // 2) % 2, (kt % 2) * SEQ:(kt % 2) * SEQ + SEQ],
                                         ACT.Copy, scale=chan_sb[:, C_NORM + phase * KT + kt:C_NORM + phase * KT + kt + 1]
                                         ).then_inc(x_hi, 1)
                row_squares(phase)

            def row_squares(phase):
                if phase:
                    act.wait_ge(h_added, 4 * phase)
                for t in range(TOKS):
                    if phase or t:
                        act.wait_ge(squares_done, TOKS * phase + t)
                    nc.scalar.activation(squares[:, :], h[:, t, :], ACT.Square,
                                         accum_out=sumsq[:, t:t + 1]).then_inc(squares_done, 1)

            def ffn(f):
                phase, u0 = PHASE_OF_FFN[f], U_FFN[f]
                g0 = f * CHUNKS

                def silu(n):
                    done = u0 + 2 if isinstance(n, int) and n == 0 else u0 + 3 * n + 1
                    act.wait_ge(unit_used, done)
                    for t in range(TOKS):
                        nc.scalar.activation(silu_g[:, t, :], ps[:, GU + t, 0:256], ACT.Silu,
                                             scale=rstd[:, t:t + 1]).then_inc(silu_done, 1)

                def high_of_gated(n):
                    act.wait_ge(g_trans, g0 + n + 1)
                    nc.scalar.copy(ghi[:, :, :].rearrange("p a b -> p (a b)"), ps[:, TR, :]).then_inc(g_hi, 1)

                if f == 0:
                    for u in range(SLOTS - 1):
                        convert(u)
                    act.wait_ge(loaded, LOADS)
                norm_in(phase)
                convert(u0 + 2)
                act.wait_ge(rstd_ready, phase + 1)
                convert(u0 + 3)
                silu(0)
                convert(u0 + 4)
                with act.Fori(1, CHUNKS - 1) as n:
                    high_of_gated(n - 1)
                    convert_in_loop(u0, n, 2)
                    silu(n)
                    convert_in_loop(u0, n, 3)
                    convert_in_loop(u0, n, 4)
                n = CHUNKS - 1
                high_of_gated(n - 1)
                convert(u0 + 3 * n + 2)
                silu(n)
                convert(u0 + 3 * n + 3)
                convert(u0 + 3 * n + 4)
                high_of_gated(n)

            def conv():
                norm_in(1)
                convert(U_CONV + 2)
                act.wait_ge(const_made, 2)
                for c in range(CV_CHUNKS):
                    u = U_CONV + 2 * c
                    convert(u + 3)
                    if c >= 1:
                        channels_in(act, c - 1)
                    for t in range(TOKS):
                        act.wait_ge(cv_bias, 2 * c + t + 1)
                        nc.scalar.activation(sg[:, t, :], ag[:, t, 256:512], ACT.Sigmoid).then_inc(cv_sig, 1)
                    convert(u + 4)
                channels_in(act, CV_CHUNKS - 1)
                for i in range(DW_PE):
                    act.wait_ge(dw_pe, i + 1)
                    nc.scalar.activation(cvo[:, DW_DVE + i, :], ps[:, 4 + i, 0:SEQ], ACT.Identity,
                                         bias=chan_sb[:, C_BDW + DW_DVE + i:C_BDW + DW_DVE + i + 1]).then_inc(dw_out, 1)
                for j in range(4):
                    act.wait_ge(centred, j + 1)
                    nc.scalar.activation(cvs[:, 2 * j:2 * j + 2, :], cvo[:, 2 * j:2 * j + 2, :],
                                         ACT.Square).then_inc(cv_squares, 1)
                act.wait_ge(var_done, 1)
                nc.scalar.activation(ln_std, ps[:, 7, 0:SEQ], ACT.Sqrt, bias=eps_sb[:, 0:1]).then_inc(std_done, 1)
                for j in range(4):
                    act.wait_ge(normed, j + 1)
                    for ct in (2 * j, 2 * j + 1):
                        nc.scalar.activation(cvs[:, ct, :], cvo[:, ct, :], ACT.Silu,
                                             bias=chan_sb[:, C_LNB + ct:C_LNB + ct + 1],
                                             scale=chan_sb[:, C_LNG + ct:C_LNG + ct + 1]).then_inc(cv_act, 1)
                    act.wait_ge(cv_act, 2 * j + 2)
                    nc.scalar.copy(xhi[:, 2 * j:2 * j + 2, :], cvs[:, 2 * j:2 * j + 2, :]).then_inc(z_hi, 1)
                convert(U_CONV + 11)
                convert(U_CONV + 12)
                convert(U_CONV + 13)

            def channels_in(eng, c):
                eng.wait_ge(cv_trans, c + 1)
                if c == 0:
                    eng.wait_ge(hb_zero, 1)
                nc.scalar.copy(hb[:, 2 * c:2 * c + 2, PAD:PAD + SEQ],
                               ps[:, TR + c % 2, :].rearrange("p (a b) -> p a b", a=2)).then_inc(hb_ready, 1)

            def gla():
                U = U_GLA
                norm_in(4)
                convert(U + 2)
                act.wait_ge(rstd_ready, 5)
                act.wait_ge(za_done, 1)
                for t in range(TOKS):
                    nc.scalar.activation(za[:, t, :], ps[:, 4, t * 16:t * 16 + 16], ACT.Copy,
                                         scale=rstd[:, t:t + 1]).then_inc(za_scaled, 1)
                convert(U + 3)

                def scaled(k, bank, dst, c0, signal):
                    act.wait_ge(unit_used, U + k + 1)
                    for t in range(TOKS):
                        nc.scalar.activation(dst[:, t, c0:c0 + 512], ps[:, bank + t, :], ACT.Copy,
                                             scale=rstd[:, t:t + 1]).then_inc(signal, 1)

                scaled(1, 0, q_tok, 0, qk_tok)
                convert(U + 4)
                act.wait_ge(za_trans, 1)
                nc.scalar.copy(aT[0:16, :], ps[0:16, 5, 0:SEQ]).then_inc(aT_ready, 1)
                convert(U + 5)
                act.wait_ge(zb_ready, HEADS)
                nc.scalar.activation(dif0, zb, ACT.Abs).then_inc(soft, 1)
                act.wait_ge(soft, 1)
                nc.scalar.activation(dif1, dif0, ACT.Exp, scale=-1.0).then_inc(soft, 1)
                act.wait_ge(soft, 2)
                nc.scalar.activation(dif0, dif1, ACT.Ln, bias=1.0).then_inc(soft, 1)
                convert(U + 6)
                scaled(3, 2, k_tok, 0, qk_tok)
                for b in range(2):
                    act.wait_ge(qk_trans, b + 1)
                    nc.scalar.mul(qT[:, 2 * b:2 * b + 2, :], ps[:, TR + b, :].rearrange("p (a b) -> p a b", a=2),
                                  HK ** -0.5).then_inc(qkT_ready, 1)
                convert(U + 7)
                for b in range(2):
                    act.wait_ge(qk_trans, 2 + b + 1)
                    nc.scalar.copy(kT[:, 2 * b:2 * b + 2, :],
                                   ps[:, TR + b, :].rearrange("p (a b) -> p a b", a=2)).then_inc(qkT_ready, 1)
                convert(U + 8)

                def decay(lv):
                    act.wait_ge(dif_ready, 2 * (lv + 1))
                    nc.scalar.activation(dif[lv % 2], dif[lv % 2], ACT.Exp, scale=1.0 / TAU).then_inc(decay_ready, 1)

                def r_gate(c):
                    act.wait_ge(r_biased, 2 * (c + 1))
                    nc.scalar.activation(rg[:, :, c * 512:c * 512 + 512], rg[:, :, c * 512:c * 512 + 512],
                                         ACT.Silu).then_inc(r_silu, 1)

                decay(0)
                decay(1)
                convert(U + 9)
                decay(2)
                decay(3)
                convert(U + 10)
                decay(4)
                convert(U + 11)
                decay(5)
                convert(U + 12)
                scaled(9, 0, v_sb, 0, v_ready)
                decay(6)
                convert(U + 13)
                decay(7)
                convert(U + 14)
                scaled(11, 2, v_sb, 512, v_ready)
                r_gate(0)
                r_gate(1)
                act.wait_ge(scores, 2 * HEADS + 1)
                nc.scalar.copy(attn[:, :, :].rearrange("p (a b) c -> p a b c", b=3)[:, :, 2, :],
                               ps[:, 4, :].rearrange("p (a b) -> p a b", a=HEADS)).then_inc(attn_ready, 1)
                for hd in range(HEADS):
                    act.wait_ge(o_done, 2 * (hd // 2) + 2)
                    for t in range(TOKS):
                        if hd or t:
                            act.wait_ge(o_squares, 2 * hd + t)
                        nc.scalar.activation(masked[0][:, 0:2, :].rearrange("p a b -> p (a b)"),
                                             ps[:, 2 * t + hd // 2, (hd % 2) * HV:(hd % 2) * HV + HV], ACT.Square,
                                             accum_out=o_ss[:, 2 * hd + t:2 * hd + t + 1]).then_inc(o_squares, 1)
                for j in range(4):
                    act.wait_ge(y_trans, j + 1)
                    nc.scalar.copy(xhi[:, 2 * j:2 * j + 2, :],
                                   ps[:, TR + j % 2, :].rearrange("p (a b) -> p a b", a=2)).then_inc(y_hi, 1)
                convert(U + 15)
                convert(U + 16)
                convert(U + 17)

            ffn(0)
            conv()
            ffn(1)
            ffn(2)
            gla()
            ffn(3)
            row_squares(6)

        @block.vector
        def _(dve):
            def low(slot):
                nc.vector.tensor_tensor(wlo[:, slot, :], raw[:, slot, :], whi[:, slot, :].bitcast(F32),
                                        ALU.subtract).then_inc(lo_made, 1)

            def convert(u):
                if u >= UNITS:
                    return
                dve.wait_ge(hi_made, u + 1)
                low(u % SLOTS)

            def convert_in_loop(u0, n, k):
                dve.wait_ge(hi_made, u0 + 3 * n + k + 1)
                low((u0 + k) % SLOTS)

            def norm_in(phase):
                for kt in range(KT):
                    if kt % 2 == 0:
                        dve.wait_ge(x_hi, KT * phase + kt + 2)
                    nc.vector.scalar_tensor_tensor(
                        out=xlo[:, kt, :], in0=ps[:, TR + (kt // 2) % 2, (kt % 2) * SEQ:(kt % 2) * SEQ + SEQ],
                        scalar=chan_sb[:, C_NORM + phase * KT + kt:C_NORM + phase * KT + kt + 1],
                        in1=xhi[:, kt, :].bitcast(F32), op0=ALU.mult, op1=ALU.subtract).then_inc(x_lo, 1)

            def residual(phase, factor, last_unit):
                for half in range(2):
                    if half == 0:
                        dve.wait_ge(down_half, phase + 1)
                    else:
                        dve.wait_ge(unit_used, last_unit + 1)
                    for t in range(TOKS):
                        c = slice(half * 512, half * 512 + 512)
                        nc.vector.scalar_tensor_tensor(out=h[:, t, c], in0=ps[:, DN + 2 * t + half, :], scalar=factor,
                                                       in1=h[:, t, c], op0=ALU.mult, op1=ALU.add).then_inc(h_added, 1)

            def ffn(f):
                phase, u0 = PHASE_OF_FFN[f], U_FFN[f]
                g0 = f * CHUNKS

                def gate(n):
                    for t in range(TOKS):
                        dve.wait_ge(silu_done, 2 * (g0 + n) + t + 1)
                        nc.vector.scalar_tensor_tensor(out=gated[:, t, :], in0=ps[:, GU + t, 256:512],
                                                       scalar=rstd[:, t:t + 1], in1=silu_g[:, t, :],
                                                       op0=ALU.mult, op1=ALU.mult).then_inc(gated_done, 1)

                def low_of_gated(n):
                    dve.wait_ge(g_hi, g0 + n + 1)
                    nc.vector.tensor_tensor(glo[:, :, :].rearrange("p a b -> p (a b)"), ps[:, TR, :],
                                            ghi[:, :, :].rearrange("p a b -> p (a b)").bitcast(F32),
                                            ALU.subtract).then_inc(g_lo, 1)

                if f == 0:
                    for u in range(SLOTS - 1):
                        convert(u)
                norm_in(phase)
                convert(u0 + 2)
                convert(u0 + 3)
                gate(0)
                convert(u0 + 4)
                with dve.Fori(1, CHUNKS - 1) as n:
                    low_of_gated(n - 1)
                    convert_in_loop(u0, n, 2)
                    gate(n)
                    convert_in_loop(u0, n, 3)
                    convert_in_loop(u0, n, 4)
                n = CHUNKS - 1
                low_of_gated(n - 1)
                convert(u0 + 3 * n + 2)
                gate(n)
                convert(u0 + 3 * n + 3)
                convert(u0 + 3 * n + 4)
                low_of_gated(n)
                residual(phase, 0.5, u0 + FFN_UNITS - 1)

            def conv():
                norm_in(1)
                convert(U_CONV + 2)
                dve.wait_ge(rstd_ready, 2)
                dve.wait_ge(bias_loaded, 32)
                for c in range(CV_CHUNKS):
                    u = U_CONV + 2 * c
                    convert(u + 3)
                    dve.wait_ge(unit_used, u + 2)
                    for t in range(TOKS):
                        if c:
                            dve.wait_ge(cv_gated, 2 * (c - 1) + t + 1)
                        nc.vector.scalar_tensor_tensor(out=ag[:, t, :], in0=ps[:, 2 * (c % 2) + t, :],
                                                       scalar=rstd[:, t:t + 1], in1=cvb[:, c * 512:c * 512 + 512],
                                                       op0=ALU.mult, op1=ALU.add).then_inc(cv_bias, 1)
                    if c:
                        dve.wait_ge(cv_trans, c)
                    for t in range(TOKS):
                        dve.wait_ge(cv_sig, 2 * c + t + 1)
                        nc.vector.tensor_tensor(gated[:, t, :], ag[:, t, 0:256], sg[:, t, :],
                                                ALU.mult).then_inc(cv_gated, 1)
                    convert(u + 4)
                for ct in range(DW_DVE):
                    dve.wait_ge(hb_ready, ct // 2 + 1)
                    nc.vector.tensor_scalar(cvo[:, ct, :], hb[:, ct, 0:SEQ],
                                            chan_sb[:, C_DW + ct * TAPS:C_DW + ct * TAPS + 1],
                                            chan_sb[:, C_BDW + ct:C_BDW + ct + 1], ALU.mult, ALU.add).then_inc(dw_step, 1)
                with dve.Fori(1, TAPS) as j:
                    for ct in range(DW_DVE):
                        dve.wait_ge(dw_step, (j - 1) * DW_DVE + ct + 1)
                        nc.vector.scalar_tensor_tensor(out=cvo[:, ct, :], in0=hb[:, ct, bass.ds(j, SEQ)],
                                                       scalar=chan_sb[:, bass.ds(j + (C_DW + ct * TAPS), 1)],
                                                       in1=cvo[:, ct, :], op0=ALU.mult, op1=ALU.add).then_inc(dw_step, 1)
                dve.wait_ge(mean_done, 1)
                for j in range(4):
                    nc.vector.tensor_tensor(cvo[:, 2 * j:2 * j + 2, :], cvo[:, 2 * j:2 * j + 2, :],
                                            ps[:, 6, 0:SEQ].unsqueeze(1).to_broadcast([P, 2, SEQ]),
                                            ALU.subtract).then_inc(centred, 1)
                dve.wait_ge(std_done, 1)
                nc.vector.reciprocal(ln_rstd, ln_std).then_inc(ln_rstd_done, 1)
                dve.wait_ge(ln_rstd_done, 1)
                for j in range(4):
                    nc.vector.tensor_tensor(cvo[:, 2 * j:2 * j + 2, :], cvo[:, 2 * j:2 * j + 2, :],
                                            ln_rstd.unsqueeze(1).to_broadcast([P, 2, SEQ]),
                                            ALU.mult).then_inc(normed, 1)
                for j in range(4):
                    dve.wait_ge(z_hi, j + 1)
                    nc.vector.tensor_tensor(xlo[:, 2 * j:2 * j + 2, :], cvs[:, 2 * j:2 * j + 2, :],
                                            xhi[:, 2 * j:2 * j + 2, :].bitcast(F32), ALU.subtract).then_inc(z_lo, 1)
                convert(U_CONV + 11)
                convert(U_CONV + 12)
                convert(U_CONV + 13)
                dve.wait_ge(bias_added, 1)
                residual(1, 1.0, U_CONV + CV_UNITS - 1)

            def gla():
                U = U_GLA
                norm_in(4)
                convert(U + 2)
                convert(U + 3)
                convert(U + 4)
                convert(U + 5)
                dve.wait_ge(a2_done, 1)
                for hd in range(HEADS):
                    nc.vector.tensor_scalar(zb[:, hd, :], ps[:, 4 + hd // 2, (hd % 2) * SEQ:(hd % 2) * SEQ + SEQ],
                                            chan_sb[:, C_BA + hd:C_BA + hd + 1], None, ALU.add).then_inc(zb_ready, 1)
                dve.wait_ge(soft, 3)
                nc.vector.scalar_tensor_tensor(out=zb, in0=zb, scalar=0.0, in1=dif0,
                                               op0=ALU.min, op1=ALU.subtract).then_inc(la_ready, 1)
                convert(U + 6)
                dve.wait_ge(keep_ready, 3)
                dve.wait_ge(la_ready, 1)
                for hd in range(HEADS):
                    nc.vector.tensor_tensor_scan(b64[:, hd, :], keep64, zb[:, hd, :], 0.0,
                                                 ALU.mult, ALU.add).then_inc(scanned, 1)
                    nc.vector.tensor_tensor_scan(b256[:, hd, :], keep_all, zb[:, hd, :], 0.0,
                                                 ALU.mult, ALU.add).then_inc(scanned, 1)
                convert(U + 7)
                convert(U + 8)
                dve.wait_ge(scanned, 2 * HEADS)
                dve.wait_ge(rstd_ready, 5)

                def difference(lv):
                    m = 2 ** lv
                    b = b64 if m <= 32 else b256
                    bv = b.rearrange("p a b -> p (a b)").rearrange("p (g two m) -> p g two m", two=2, m=m)
                    dv = dif[lv % 2].rearrange("p a b -> p (a b)").rearrange("p (g two m) -> p g two m", two=2, m=m)
                    groups = HEADS * SEQ // (2 * m)
                    mid = bv[:, :, 0, m - 1:m].to_broadcast([P, groups, m])
                    if lv >= 2:
                        dve.wait_ge(qk_ready, 2 * (lv - 1))
                    nc.vector.tensor_tensor(dv[:, :, 0, :], mid, bv[:, :, 0, :], ALU.subtract).then_inc(dif_ready, 1)
                    nc.vector.tensor_tensor(dv[:, :, 1, :], bv[:, :, 1, :], mid, ALU.subtract).then_inc(dif_ready, 1)

                def r_bias(c):
                    dve.wait_ge(unit_used, U + 5 + 2 * c + 1)
                    for t in range(TOKS):
                        nc.vector.scalar_tensor_tensor(out=rg[:, t, c * 512:c * 512 + 512], in0=ps[:, 2 * c + t, :],
                                                       scalar=rstd[:, t:t + 1], in1=rows_sb[:, c * 512:c * 512 + 512],
                                                       op0=ALU.mult, op1=ALU.add).then_inc(r_biased, 1)

                difference(0)
                difference(1)
                convert(U + 9)
                r_bias(0)
                difference(2)
                difference(3)
                convert(U + 10)
                difference(4)
                r_bias(1)
                convert(U + 11)
                difference(5)
                convert(U + 12)
                difference(6)
                convert(U + 13)
                difference(7)
                convert(U + 14)
                dve.wait_ge(loaded, LOADS)
                for i in range(2 * HEADS):
                    hd, tile = i // 2, i % 2
                    bank = 4 + 2 * (i % 2)
                    dve.wait_ge(scores, i + 1)
                    if i >= 2:
                        dve.wait_ge(attn_ready, i - 1)
                    mk = masked[i % 2]
                    nc.vector.tensor_tensor(mk, ps[:, bank:bank + 2, :].rearrange("p a (l t) -> p (a l) t", t=P),
                                            mask_sb[:, :, :], ALU.mult).then_inc(masked_ready, 1)
                    dve.wait_ge(masked_ready, i + 1)
                    if i == 0:
                        dve.wait_ge(qk_ready, 2 * LEVELS)
                    nc.vector.tensor_reduce(attn[:, 3 * hd + tile, :], mk.rearrange("p l t -> p t l"),
                                            AX_X, ALU.add).then_inc(attn_ready, 1)
                dve.wait_ge(o_rstd_done, 1)
                dve.wait_ge(rg_ready, 2)
                for hd in range(HEADS):
                    for t in range(TOKS):
                        c = slice(hd * HV, hd * HV + HV)
                        nc.vector.scalar_tensor_tensor(
                            out=y_tok[:, t, c], in0=ps[:, 2 * t + hd // 2, (hd % 2) * HV:(hd % 2) * HV + HV],
                            scalar=o_rstd[:, 2 * hd + t:2 * hd + t + 1], in1=rg[:, t, c],
                            op0=ALU.mult, op1=ALU.mult).then_inc(y_ready, 1)
                for j in range(4):
                    dve.wait_ge(y_hi, j + 1)
                    nc.vector.tensor_tensor(xlo[:, 2 * j:2 * j + 2, :],
                                            ps[:, TR + j % 2, :].rearrange("p (a b) -> p a b", a=2),
                                            xhi[:, 2 * j:2 * j + 2, :].bitcast(F32), ALU.subtract).then_inc(y_lo, 1)
                convert(U + 15)
                convert(U + 16)
                convert(U + 17)
                residual(4, 1.0, U + GLA_UNITS - 1)

            ffn(0)
            conv()
            ffn(1)
            ffn(2)
            gla()
            ffn(3)
            dve.wait_ge(rstd_ready, 7)
            dve.wait_ge(gain_loaded, 16)
            for t in range(TOKS):
                nc.vector.scalar_tensor_tensor(out=h[:, t, :], in0=h[:, t, :], scalar=rstd[:, t:t + 1],
                                               in1=pair[:, :], op0=ALU.mult, op1=ALU.mult).then_inc(out_ready, 1)

        @block.gpsimd
        def _(pool):
            nc.gpsimd.memset(mean_w[:, :], 1.0 / D).then_inc(const_made, 1)
            nc.gpsimd.memset(eps_sb[:, :], EPS).then_inc(const_made, 1)
            nc.gpsimd.memset(neg_half[:, :], -0.5).then_inc(const_made, 1)
            nc.gpsimd.memset(hb[:, :, 0:PAD], 0.0).then_inc(hb_zero, 1)

            def row_rstd(phase):
                pool.wait_ge(squares_done, TOKS * (phase + 1))
                nc.gpsimd.tensor_scalar(ms[:, :], sumsq[:, :], 1.0 / D, EPS, ALU.mult, ALU.add).then_inc(ms_done, 1)
                pool.wait_ge(ms_done, phase + 1)
                nc.gpsimd.tensor_tensor(rstd[:, :], ms[:, :], neg_half[:, 0:TOKS], ALU.pow).then_inc(rstd_ready, 1)

            pool.wait_ge(const_made, 3)
            row_rstd(0)
            pool.wait_ge(loaded, LOADS)
            for i in range(DW_PE):
                ct = DW_DVE + i
                nc.gpsimd.tensor_tensor(diag[:, i, :, :], ident[:, :].unsqueeze(1).to_broadcast([P, TAPS, P]),
                                        chan_sb[:, C_DW + ct * TAPS:C_DW + (ct + 1) * TAPS].unsqueeze(2)
                                        .to_broadcast([P, TAPS, P]), ALU.mult).then_inc(diag_made, 1)
            nc.gpsimd.tensor_copy(a1_hi[:, :], a1_raw[:, :]).then_inc(a1_split, 1)
            pool.wait_ge(a1_split, 1)
            nc.gpsimd.tensor_tensor(a1_lo[:, :], a1_raw[:, :], a1_hi[:, :].bitcast(F32),
                                    ALU.subtract).then_inc(a1_split, 1)
            row_rstd(1)
            pool.wait_ge(bias_loaded, 32)
            pool.wait_ge(x_trans, 8)
            nc.gpsimd.tensor_tensor(h[:, :, :], h[:, :, :],
                                    cvb[:, 2 * D:3 * D].unsqueeze(1).to_broadcast([P, TOKS, D]),
                                    ALU.add).then_inc(bias_added, 1)
            row_rstd(2)
            row_rstd(3)
            row_rstd(4)
            nc.gpsimd.memset(keep64, 1.0).then_inc(keep_ready, 1)
            nc.gpsimd.memset(keep_all, 1.0).then_inc(keep_ready, 1)
            pool.wait_ge(keep_ready, 1)
            nc.gpsimd.memset(keep64.rearrange("p (c t) -> p c t", t=64)[:, :, 0:1], 0.0).then_inc(keep_ready, 1)
            for lv in range(LEVELS):
                m = 2 ** lv
                pool.wait_ge(decay_ready, lv + 1)
                if lv == 0:
                    pool.wait_ge(qkT_ready, 4)
                split = "p (g two m) -> p g two m"
                dv = dif[lv % 2].rearrange("p a b -> p (a b)").rearrange(split, two=2, m=m)
                ov = qk[:, lv, :].rearrange(split, two=2, m=m)
                for part, src in ((0, kT), (1, qT)):
                    sv = src.rearrange("p a b -> p (a b)").rearrange(split, two=2, m=m)
                    nc.gpsimd.tensor_tensor(ov[:, :, part, :], dv[:, :, part, :], sv[:, :, part, :],
                                            ALU.mult).then_inc(qk_ready, 1)
            for c in range(2):
                pool.wait_ge(r_silu, c + 1)
                for t in range(TOKS):
                    rv = rg[:, t, c * 512:c * 512 + 512].rearrange("p (a b) -> p a b", b=HV)
                    ins = nc.gpsimd.tensor_tensor(rv, rv, rows_sb[:, D:D + HV].unsqueeze(1)
                                                  .to_broadcast([P, 2, HV]), ALU.mult)
                ins.then_inc(rg_ready, 1)
            pool.wait_ge(o_squares, 2 * HEADS)
            nc.gpsimd.tensor_scalar(o_ms, o_ss, 1.0 / HV, EPS, ALU.mult, ALU.add).then_inc(o_ms_done, 1)
            pool.wait_ge(o_ms_done, 1)
            nc.gpsimd.tensor_tensor(o_rstd, o_ms, neg_half[:, :], ALU.pow).then_inc(o_rstd_done, 1)
            row_rstd(5)
            row_rstd(6)


INS = ["stream", "x", "chan", "rows", "a1", "a2", "masks", "ident"]


def level_masks():
    s, t = np.arange(P)[:, None], np.arange(P)[None, :]
    out = [s == t]
    for lv in range(LEVELS - 1):
        m = 2 ** lv
        out.append((s // (2 * m) == t // (2 * m)) & (s // m % 2 == 0) & (t // m % 2 == 1))
    return np.stack(out, axis=1).astype(np.float32).reshape(P, LEVELS * P)


def kernel(**inputs):
    import concourse.bacc as _bacc
    from concourse.bass_utils import run_bass_kernel_spmd as _run

    a = {k: np.asarray(v) for k, v in inputs.items()}

    def wide(left, right, chunk):
        n = left.shape[1] // chunk
        both = [w.reshape(2, 4, P, n, chunk) for w in (left, right)]
        both = np.concatenate(both, axis=4)
        return both.transpose(3, 0, 2, 1, 4).reshape(2 * n, P, UNIT)

    def single(w):
        return w.reshape(2, 4, P, w.shape[1] // 512, 512).transpose(3, 0, 2, 1, 4).reshape(-1, P, UNIT)

    def down(w):
        return w.reshape(-1, 2, P, D).transpose(0, 2, 1, 3).reshape(-1, P, UNIT)

    def ffn(name, i):
        gu = wide(a[name + "_gate"][i], a[name + "_up"][i], 256).reshape(CHUNKS, 2, P, UNIT)
        dn = down(a[name + "_down"][i])
        parts = [gu[0]]
        for n in range(1, CHUNKS):
            parts += [gu[n], dn[n - 1:n]]
        return np.concatenate(parts + [dn[CHUNKS - 1:]])

    pw1 = a["cv_w_pw1"][0]
    stream = np.concatenate([
        ffn("w1", 0), wide(pw1[:, :D], pw1[:, D:], 256), down(a["cv_w_pw2"][0]), ffn("w2", 0), ffn("w1", 1),
        single(a["gla_w_q"][0]), single(a["gla_w_k"][0]), single(a["gla_w_r"][0]), single(a["gla_w_v"][0]),
        down(a["gla_w_o"][0]), ffn("w2", 1)])

    def col(v):
        return v.reshape(-1, P).T

    norms = [a["g_ffn1"][0], a["g_mix"][0], a["g_ffn2"][0], a["g_ffn1"][1], a["g_mix"][1], a["g_ffn2"][1]]
    dw = a["cv_w_dw"][0].reshape(TAPS, KT, P).transpose(2, 1, 0).reshape(P, KT * TAPS)
    chan = np.concatenate([col(v) for v in norms] + [dw, col(a["cv_b_dw"][0]), col(a["cv_ln_g"][0]),
                                                     col(a["cv_ln_b"][0]), col(a["gla_b_a"][0])], axis=1)
    bpw1 = a["cv_b_pw1"][0].reshape(2, CV_CHUNKS, 256).transpose(1, 0, 2).reshape(-1)
    rows = np.concatenate([bpw1, a["cv_b_pw2"][0], a["gla_b_r"][0], a["gla_norm_g"][0], a["g_final"]])
    arrays = {
        "stream": stream, "x": a["x"], "chan": chan, "rows": rows,
        "a1": a["gla_w_a1"][0].reshape(KT, P, 16).transpose(1, 0, 2).reshape(P, KT * 16),
        "a2": a["gla_w_a2"][0], "masks": level_masks(), "ident": np.eye(P, dtype=np.float32),
    }
    arrays = {f"in_{k}_dram": np.ascontiguousarray(v) for k, v in arrays.items()}
    nc = _bacc.Bacc("TRN2", target_bir_lowering=False, num_devices=1)
    args = [nc.dram_tensor(f"in_{k}_dram", arrays[f"in_{k}_dram"].shape, mybir.dt.float32, kind="ExternalInput").ap()
            for k in INS]
    out = nc.dram_tensor("out_0_dram", (1, SEQ, D), mybir.dt.float32, kind="ExternalOutput").ap()
    build(nc, *args, out)
    r = _run(nc, [arrays], core_ids=[0])
    return r.results[0]["out_0_dram"]
```

```python
from contextlib import ExitStack

import numpy as np

import concourse.bass as bass
from concourse import mybir
from concourse.alu_op_type import AluOpType as ALU

F32 = mybir.dt.float32
F32R = mybir.dt.float32r
ACT = mybir.ActivationFunctionType
AX_X = mybir.AxisListType.X

P = 128
D = 1024
SEQ = 256
FF = 2816
TOKS = SEQ // P
KT = D // P
EPS = 1e-6
UNIT = 2048
SLOTS = 3
CHUNKS = FF // 256
FFN_UNITS = 3 * CHUNKS
TAPS = 31
PAD = TAPS - 1
CV_CHUNKS = D // 256
CV_UNITS = 2 * CV_CHUNKS + 4
HEADS = 4
HK = 128
HV = 256
TAU = 16.0
LEVELS = 8
GLA_UNITS = 16

U_FFN = [0, FFN_UNITS + CV_UNITS, 2 * FFN_UNITS + CV_UNITS, 3 * FFN_UNITS + CV_UNITS + GLA_UNITS]
U_CONV = FFN_UNITS
U_GLA = 3 * FFN_UNITS + CV_UNITS
UNITS = U_FFN[3] + FFN_UNITS
PHASE_OF_FFN = [0, 2, 3, 5]

DW_DVE = 5
DW_PE = KT - DW_DVE

C_NORM = 0
C_DW = C_NORM + 6 * KT
C_BDW = C_DW + KT * TAPS
C_LNG = C_BDW + KT
C_LNB = C_LNG + KT
C_BA = C_LNB + KT
C_END = C_BA + HEADS
R_BPW1 = 0
R_BPW2 = R_BPW1 + 2 * D
R_BR = R_BPW2 + D
R_NG = R_BR + D
R_GF = R_NG + HV
R_END = R_GF + D
SCORES = LEVELS * P



def build(nc, stream, x, chan, rows, a1, a2, masks, ident_d, out):
    with ExitStack() as ctx:
        def sb(name, shape, dt=F32):
            return ctx.enter_context(nc.sbuf_tensor(name, shape, dt))

        def sem(name):
            return ctx.enter_context(nc.semaphore(name))

        ps = ctx.enter_context(nc.psum_tensor("ps", [P, 8, 512], F32))
        GU, DN, TR = 0, 2, 6
        DW_BANKS = [4, 5, 0]

        h = sb("h", [P, TOKS, D])
        raw = sb("raw", [P, SLOTS, UNIT])
        whi = sb("whi", [P, SLOTS, UNIT], F32R)
        wlo = sb("wlo", [P, SLOTS, UNIT], F32R)
        xhi = sb("xhi", [P, KT, SEQ], F32R)
        xlo = sb("xlo", [P, KT, SEQ], F32R)
        ghi = sb("ghi", [P, 2, SEQ], F32R)
        glo = sb("glo", [P, 2, SEQ], F32R)
        pair = sb("pair", [P, D])
        silu_g = pair[:, 0:512].rearrange("p (t c) -> p t c", t=TOKS)
        gated = pair[:, 512:1024].rearrange("p (t c) -> p t c", t=TOKS)
        squares = sb("squares", [P, D])
        chan_sb = sb("chan_sb", [P, C_END])
        rows_sb = sb("rows_sb", [P, R_GF - R_BR])
        ident = sb("ident", [P, P])
        a1_hi = sb("a1_hi", [P, KT * 16], F32R)
        a1_lo = sb("a1_lo", [P, KT * 16], F32R)
        mean_w = sb("mean_w", [P, P])
        sumsq = sb("sumsq", [P, TOKS])
        ms = sb("ms", [P, TOKS])
        rstd = sb("rstd", [P, TOKS])
        neg_half = sb("neg_half", [P, TOKS * HEADS])
        eps_sb = sb("eps_sb", [P, 1])
        WORK = 22912
        work = sb("work", [P, WORK])

        def area(at, *shape):
            n = int(np.prod(shape))
            v = work[:, at:at + n]
            assert at + n <= WORK, (at, n)
            if len(shape) == 2:
                v = v.rearrange("p (a b) -> p a b", a=shape[0])
            if len(shape) == 3:
                v = v.rearrange("p (a b c) -> p a b c", a=shape[0], b=shape[1])
            return v, at + n

        diag, at = area(0, DW_PE, TAPS, P)
        hb, at = area(at, KT, PAD + SEQ)
        cvo, at = area(at, KT, SEQ)
        cvs, at = area(at, KT, SEQ)
        ln_at = at
        ag, at = area(at, TOKS, 512)
        sg, at = area(at, TOKS, 256)
        ln_std, ln_at = area(ln_at, SEQ)
        ln_rstd, _ = area(ln_at, SEQ)
        cvb, at = area(at, R_BR)
        q_tok = squares[:, :].rearrange("p (t c) -> p t c", t=TOKS)
        k_tok = pair[:, :].rearrange("p (t c) -> p t c", t=TOKS)
        qT, at = area(0, HEADS, SEQ)
        kT, at = area(at, HEADS, SEQ)
        v_sb, at = area(at, TOKS, D)
        rg, at = area(at, TOKS, D)
        y_at = at
        zb, at = area(at, HEADS, SEQ)
        dif0, at = area(at, HEADS, SEQ)
        dif1, at = area(at, HEADS, SEQ)
        b64, at = area(at, HEADS, SEQ)
        b256, at = area(at, HEADS, SEQ)
        qk, at = area(at, LEVELS, HEADS * SEQ)
        keep64, at = area(at, SEQ)
        keep_all, at = area(at, SEQ)
        za, at = area(at, TOKS, 16)
        aT, at = area(at, SEQ)
        o_ss, at = area(at, 8)
        o_ms, at = area(at, 8)
        o_rstd, at = area(at, 8)
        mask_sb, at = area(at, LEVELS, P)
        a1_raw, at = area(at, KT * 16)
        a2_sb, at = area(at, HEADS * HK)
        a2_sb = a2_sb[0:16, :]
        dif = [dif0, dif1]
        masked = [squares[:, :].rearrange("p (l t) -> p l t", l=LEVELS),
                  pair[:, :].rearrange("p (l t) -> p l t", l=LEVELS)]
        y_tok, at2 = area(y_at, TOKS, D)
        attn, at2 = area(at2, HEADS * 3, P)

        x_loaded = [sem(f"x_loaded{t}") for t in range(TOKS)]
        ident_loaded = sem("ident_loaded")
        chan_loaded = sem("chan_loaded")
        gla_loaded = sem("gla_loaded")
        piece_landed = [sem(f"piece_landed{k}") for k in range(3)]
        hi_piece = sem("hi_piece")
        lo_piece = sem("lo_piece")
        bias_loaded = sem("bias_loaded")
        gain_loaded = sem("gain_loaded")
        raw_landed = [sem(f"raw_landed{s}") for s in range(SLOTS)]
        pieces = piece_landed + [raw_landed[0]]
        hi_made = sem("hi_made")
        lo_made = sem("lo_made")
        unit_used = sem("unit_used")
        h_added = sem("h_added")
        x_trans = sem("x_trans")
        x_hi = sem("x_hi")
        x_lo = sem("x_lo")
        squares_done = sem("squares_done")
        ms_done = sem("ms_done")
        rstd_ready = sem("rstd_ready")
        silu_done = sem("silu_done")
        gated_done = sem("gated_done")
        g_trans = sem("g_trans")
        g_hi = sem("g_hi")
        g_lo = sem("g_lo")
        down_part = sem("down_part")
        const_made = sem("const_made")
        diag_made = sem("diag_made")
        cv_bias = sem("cv_bias")
        cv_sig = sem("cv_sig")
        cv_gated = sem("cv_gated")
        cv_trans = sem("cv_trans")
        hb_zero = sem("hb_zero")
        hb_ready = sem("hb_ready")
        dw_step = sem("dw_step")
        dw_pe = sem("dw_pe")
        dw_out = sem("dw_out")
        mean_done = sem("mean_done")
        centred = sem("centred")
        cv_squares = sem("cv_squares")
        var_done = sem("var_done")
        std_done = sem("std_done")
        ln_rstd_done = sem("ln_rstd_done")
        normed = sem("normed")
        cv_act = sem("cv_act")
        z_hi = sem("z_hi")
        z_lo = sem("z_lo")
        bias_added = sem("bias_added")
        a1_split = sem("a1_split")
        za_done = sem("za_done")
        za_scaled = sem("za_scaled")
        za_trans = sem("za_trans")
        aT_ready = sem("aT_ready")
        a2_done = sem("a2_done")
        zb_ready = sem("zb_ready")
        soft = sem("soft")
        la_ready = sem("la_ready")
        scanned = sem("scanned")
        keep_ready = sem("keep_ready")
        qk_tok = sem("qk_tok")
        v_ready = sem("v_ready")
        r_biased = sem("r_biased")
        r_silu = sem("r_silu")
        rg_ready = sem("rg_ready")
        qk_trans = sem("qk_trans")
        qkT_ready = sem("qkT_ready")
        dif_ready = sem("dif_ready")
        decay_ready = sem("decay_ready")
        qk_ready = sem("qk_ready")
        scores = sem("scores")
        masked_ready = sem("masked_ready")
        fold_a = sem("fold_a")
        fold_b = sem("fold_b")
        attn_ready = sem("attn_ready")
        o_done = sem("o_done")
        o_squares = sem("o_squares")
        o_ms_done = sem("o_ms_done")
        o_rstd_done = sem("o_rstd_done")
        y_ready = sem("y_ready")
        y_trans = sem("y_trans")
        y_hi = sem("y_hi")
        y_lo = sem("y_lo")
        out_ready = sem("out_ready")
        stored = sem("stored")

        POOL_UNITS = {U_CONV + 1, U_FFN[1] + 1, U_FFN[2] + 1, U_GLA + 1, U_FFN[3] + 1, *range(U_CONV + 3, U_CONV + 11)}

        DW_RUNS = [(0, 2, 1, 6), (0, 2, 6, 15), (0, 2, 15, 24), (0, 2, 24, TAPS), (2, DW_DVE - 2, 1, TAPS)]

        def dw_before(run):
            steps = sum(n * (b - a) for _, n, a, b in DW_RUNS[:run])
            return steps + (2 if run < 4 else DW_DVE)

        def dw_last(ct):
            run = 3 if ct < 2 else 4
            ct0, n, a, b = DW_RUNS[run]
            return dw_before(run) + n * (b - a - 1) + ct - ct0 + 1

        block = ctx.enter_context(nc.Block())

        @block.sync
        def _(sp):
            xv = x.rearrange("a (t p) d -> t p (a d)", p=P)
            for t in range(TOKS):
                sp.dma_start(h[:, t, :], xv[t, :, :]).then_inc(x_loaded[t], 16)
            for k in range(4):
                c = slice(k * 512, k * 512 + 512)
                sp.dma_start(raw[:, 0, c], stream[0, :, c]).then_inc(pieces[k], 16)
            for s in range(1, SLOTS):
                sp.dma_start(raw[:, s, :], stream[s, :, :]).then_inc(raw_landed[s], 16)

            def load(u, slot):
                sp.wait_ge(lo_made, u - SLOTS + 1)
                sp.dma_start(raw[:, slot, :], stream[bass.ds(u, 1), :, :]
                             .rearrange("a p n -> p (a n)")).then_inc(raw_landed[slot], 16)

            whole = UNITS // SLOTS
            for u in range(SLOTS, 2 * SLOTS):
                load(u, u % SLOTS)
            sp.dma_start(cvb, rows[0:R_BR].partition_broadcast(P)).then_inc(bias_loaded, 16)
            sp.dma_start(rows_sb[:, :], rows[R_BR:R_GF].partition_broadcast(P)).then_inc(bias_loaded, 16)
            with sp.Fori(2, whole) as turn:
                for slot in range(SLOTS):
                    load(turn * SLOTS + slot, slot)
            for u in range(whole * SLOTS, UNITS):
                load(u, u % SLOTS)
            sp.wait_ge(g_trans, 4 * CHUNKS)
            sp.dma_start(pair[:, :], rows[R_GF:R_END].partition_broadcast(P)).then_inc(gain_loaded, 16)
            for t in range(TOKS):
                sp.wait_ge(out_ready, t + 1)
                sp.dma_start(out.rearrange("a (t p) d -> t p (a d)", p=P)[t, :, :], h[:, t, :]).then_inc(stored, 16)
            sp.wait_ge(stored, 16 * TOKS)

        @block.tensor
        def _(pe):
            def unit_ready(u):
                pe.wait_ge(hi_made, u + 1)
                pe.wait_ge(lo_made, u + 1)

            def is_first(u):
                return isinstance(u, int) and u == 0

            NATURAL = [(0, 0), (0, 1), (1, 0), (1, 1)]
            BY_TOKENS = [(0, 0), (1, 0), (0, 1), (1, 1)]

            def three(o, xh, xl, wh, wl, first, last):
                nc.tensor.matmul(o, xh, wh, start=first, stop=False)
                nc.tensor.matmul(o, xh, wl, start=False, stop=False)
                return nc.tensor.matmul(o, xl, wh, start=False, stop=last)

            def wide_unit(u, slot, half, bank, phase=None):
                if not is_first(u):
                    unit_ready(u)
                for k in range(4):
                    kt = 4 * half + k
                    if phase is not None:
                        pe.wait_ge(x_hi, KT * phase + kt + 1)
                        pe.wait_ge(x_lo, KT * phase + kt + 1)
                        if kt + 2 < KT:
                            norm_transpose(phase, kt + 2)
                    if is_first(u):
                        pe.wait_ge(hi_piece, k + 1)
                        pe.wait_ge(lo_piece, k + 1)
                    w = slice(k * 512, k * 512 + 512)
                    for t in range(TOKS):
                        s = slice(t * P, t * P + P)
                        last = three(ps[:, bank + t, :], xhi[:, kt, s], xlo[:, kt, s],
                                     whi[:, slot, w], wlo[:, slot, w], kt == 0, kt == KT - 1)
                last.then_inc(unit_used, 1)

            def down_unit(u, slot, srch, srcl, k0, first, order=None, between=None):
                unit_ready(u)
                final = order is not None
                for n, (half, t) in enumerate(order or NATURAL):
                    if between and n in between:
                        between[n]()
                    s = slice(t * P, t * P + P)
                    for k in range(2):
                        w = slice(k * D + half * 512, k * D + half * 512 + 512)
                        last = three(ps[:, DN + 2 * t + half, :], srch[:, k0 + k, s], srcl[:, k0 + k, s],
                                     whi[:, slot, w], wlo[:, slot, w], first and k == 0, final and k == 1)
                    if final and n < 3:
                        last.then_inc(down_part, 1)
                last.then_inc(unit_used, 1)

            def turn(bank, src, c0):
                for k in range(2):
                    for t in range(TOKS):
                        last = nc.tensor.transpose(ps[:, bank, k * SEQ + t * P:k * SEQ + t * P + P],
                                                   src[:, t, c0 + k * P:c0 + k * P + P], ident[:, :])
                return last

            def norm_transpose(phase, kt):
                if phase:
                    pe.wait_ge(h_added, 4 * (phase - 1) + 2 * (kt // 4 + 1))
                if kt >= 2:
                    pe.wait_ge(x_lo, KT * phase + kt - 1)
                for t in range(TOKS):
                    if phase == 0 and kt == 0:
                        pe.wait_ge(x_loaded[t], 16)
                    at = (kt // 2) % 2 * SEQ + t * P
                    last = nc.tensor.transpose(ps[:, TR + kt % 2, at:at + P], h[:, t, kt * P:kt * P + P], ident[:, :])
                last.then_inc(x_trans, 1)

            def first_transposes(phase):
                def do():
                    norm_transpose(phase, 0)
                    norm_transpose(phase, 1)
                return do

            def ffn(f):
                phase, u0, s0 = PHASE_OF_FFN[f], U_FFN[f], U_FFN[f] % SLOTS
                g0 = f * CHUNKS

                def chunk(n, first=False, last=False):
                    u = u0 + 3 * n - 1
                    if not first:
                        pe.wait_ge(gated_done, 2 * (g0 + n))
                    wide_unit(u, (s0 + 2) % SLOTS, 0, GU)
                    if first:
                        pe.wait_ge(gated_done, 2 * (g0 + n))
                    turn(TR, gated, 0).then_inc(g_trans, 1)
                    wide_unit(u + 1, s0, 1, GU)
                    pe.wait_ge(g_hi, g0 + n)
                    pe.wait_ge(g_lo, g0 + n)
                    down_unit(u + 2, (s0 + 1) % SLOTS, ghi, glo, 0, first, between={2: last_turn} if last else None)

                def last_turn():
                    pe.wait_ge(gated_done, 2 * (g0 + CHUNKS))
                    turn(TR, gated, 0).then_inc(g_trans, 1)

                if phase:
                    pe.wait_ge(h_added, 4 * (phase - 1) + 3)
                wide_unit(u0, s0, 0, DN, phase)
                wide_unit(u0 + 1, (s0 + 1) % SLOTS, 1, DN, phase)
                chunk(1, first=True)
                with pe.Fori(2, CHUNKS - 1) as n:
                    chunk(n)
                chunk(CHUNKS - 1, last=True)
                pe.wait_ge(g_hi, g0 + CHUNKS)
                pe.wait_ge(g_lo, g0 + CHUNKS)
                down_unit(u0 + FFN_UNITS - 1, (s0 + 2) % SLOTS, xhi, xlo, KT - 2, False,
                          order=BY_TOKENS if f == 3 else NATURAL,
                          between=None if f == 3 else {3: first_transposes(phase + 1)})

            def conv():
                for c in range(CV_CHUNKS):
                    u = U_CONV + 2 * c
                    bank = 2 * (c % 2)
                    if c >= 2:
                        pe.wait_ge(cv_bias, 2 * (c - 1))
                    if c == 1:
                        pe.wait_ge(h_added, 4)
                    wide_unit(u, u % SLOTS, 0, bank, 1 if c == 0 else None)
                    if c >= 1:
                        pe.wait_ge(cv_gated, 2 * c)
                        if c >= 3:
                            pe.wait_ge(hb_ready, c - 2)
                        turn(TR + (c - 1) % 2, gated, 0).then_inc(cv_trans, 1)
                    wide_unit(u + 1, (u + 1) % SLOTS, 1, bank, 1 if c == 0 else None)
                pe.wait_ge(cv_gated, 2 * CV_CHUNKS)
                pe.wait_ge(hb_ready, CV_CHUNKS - 2)
                turn(TR + (CV_CHUNKS - 1) % 2, gated, 0).then_inc(cv_trans, 1)
                pe.wait_ge(diag_made, DW_PE)
                pe.wait_ge(hb_ready, CV_CHUNKS)
                for i in range(DW_PE):
                    for j in range(TAPS):
                        last = nc.tensor.matmul(ps[:, DW_BANKS[i], 0:SEQ], diag[:, i, j, :],
                                                hb[:, DW_DVE + i, j:j + SEQ], start=(j == 0), stop=(j == TAPS - 1))
                    last.then_inc(dw_pe, 1)
                pe.wait_ge(const_made, 1)
                order = list(range(DW_DVE, KT)) + list(range(DW_DVE))
                for n, ct in enumerate(order):
                    if ct >= DW_DVE:
                        pe.wait_ge(dw_out, ct - DW_DVE + 1)
                    else:
                        pe.wait_ge(dw_step, dw_last(ct))
                    last = nc.tensor.matmul(ps[:, 6, 0:SEQ], mean_w[:, :], cvo[:, ct, :],
                                            start=(n == 0), stop=(n == KT - 1))
                last.then_inc(mean_done, 1)
                for ct in range(KT):
                    if ct % 2 == 0:
                        pe.wait_ge(cv_squares, ct // 2 + 1)
                    last = nc.tensor.matmul(ps[:, 7, 0:SEQ], mean_w[:, :], cvs[:, ct, :],
                                            start=(ct == 0), stop=(ct == KT - 1))
                last.then_inc(var_done, 1)
                for k in range(4):
                    u = U_CONV + 2 * CV_CHUNKS + k
                    pe.wait_ge(z_hi, k + 1)
                    pe.wait_ge(z_lo, k + 1)
                    down_unit(u, u % SLOTS, xhi, xlo, 2 * k, k == 0, order=NATURAL if k == 3 else None,
                              between={3: first_transposes(2)} if k == 3 else None)

            def gla():
                def unit(k, bank, phase=None):
                    u = U_GLA + k
                    wide_unit(u, u % SLOTS, k % 2, bank, phase)

                unit(0, 0, 4)
                unit(1, 0, 4)
                pe.wait_ge(a1_split, 2)
                for t in range(TOKS):
                    s = slice(t * P, t * P + P)
                    for kt in range(KT):
                        w = slice(kt * 16, kt * 16 + 16)
                        last = three(ps[:, 4, t * 16:t * 16 + 16], xhi[:, kt, s], xlo[:, kt, s],
                                     a1_hi[:, w], a1_lo[:, w], kt == 0, kt == KT - 1)
                last.then_inc(za_done, 1)
                unit(2, 2)
                pe.wait_ge(za_scaled, TOKS)
                for t in range(TOKS):
                    last = nc.tensor.transpose(ps[0:16, 5, t * P:t * P + P], za[:, t, :], ident[:, :])
                last.then_inc(za_trans, 1)
                unit(3, 2)
                pe.wait_ge(aT_ready, 1)
                for hd in range(HEADS):
                    last = nc.tensor.matmul(ps[:, 4 + hd // 2, (hd % 2) * SEQ:(hd % 2) * SEQ + SEQ],
                                            a2_sb[:, hd * HK:hd * HK + HK], aT[0:16, :], start=True, stop=True)
                last.then_inc(a2_done, 1)
                pe.wait_ge(qk_tok, 2)
                for b in range(2):
                    turn(TR + b, q_tok, b * 256).then_inc(qk_trans, 1)
                unit(4, 0)
                pe.wait_ge(qk_tok, 4)
                for b in range(2):
                    pe.wait_ge(qkT_ready, b + 1)
                    turn(TR + b, k_tok, b * 256).then_inc(qk_trans, 1)
                unit(5, 0)
                unit(6, 2)
                unit(7, 2)
                pe.wait_ge(r_biased, 2)
                unit(8, 0)
                unit(9, 0)
                pe.wait_ge(r_biased, 4)
                unit(10, 2)
                unit(11, 2)
                pe.wait_ge(qkT_ready, 4)
                pe.wait_ge(zb_ready, HEADS)
                for i in range(2 * HEADS):
                    hd, tile = i // 2, i % 2
                    bank = 4 + 2 * (i % 2)
                    if i >= 2:
                        pe.wait_ge(masked_ready, i - 1)
                    s = slice(tile * P, tile * P + P)
                    nc.tensor.matmul(ps[:, bank, 0:P], kT[:, hd, s], qT[:, hd, s], start=True, stop=True)
                    for lv in range(1, LEVELS):
                        if i == 0:
                            pe.wait_ge(qk_ready, 2 * lv)
                        both = qk[:, lv - 1, hd * SEQ + tile * P:hd * SEQ + tile * P + P]
                        last = nc.tensor.matmul(ps[:, bank + lv // 4, (lv % 4) * P:(lv % 4) * P + P],
                                                both, both, start=True, stop=True)
                    last.then_inc(scores, 1)
                pe.wait_ge(masked_ready, 2 * HEADS - 1)
                pe.wait_ge(qk_ready, 2 * LEVELS)
                for hd in range(HEADS):
                    last = nc.tensor.matmul(ps[:, 4, hd * P:hd * P + P],
                                            qk[:, LEVELS - 1, hd * SEQ:hd * SEQ + P],
                                            qk[:, LEVELS - 1, hd * SEQ + P:hd * SEQ + SEQ], start=True, stop=True)
                last.then_inc(scores, 1)
                pe.wait_ge(v_ready, 4)
                pe.wait_ge(attn_ready, 2 * HEADS + 1)
                for hd in range(HEADS):
                    c = slice((hd % 2) * HV, (hd % 2) * HV + HV)
                    vc = slice(hd * HV, hd * HV + HV)
                    nc.tensor.matmul(ps[:, hd // 2, c], attn[:, 3 * hd, :], v_sb[:, 0, vc], start=True, stop=True)
                    nc.tensor.matmul(ps[:, 2 + hd // 2, c], attn[:, 3 * hd + 2, :], v_sb[:, 0, vc],
                                     start=True, stop=False)
                    nc.tensor.matmul(ps[:, 2 + hd // 2, c], attn[:, 3 * hd + 1, :], v_sb[:, 1, vc],
                                     start=False, stop=True).then_inc(o_done, 1)
                for j in range(4):
                    pe.wait_ge(y_ready, 2 * (j + 1))
                    if j >= 2:
                        pe.wait_ge(y_hi, j - 1)
                        pe.wait_ge(y_lo, j - 1)
                    turn(TR + j % 2, y_tok, j * 256).then_inc(y_trans, 1)
                for k in range(4):
                    u = U_GLA + 12 + k
                    pe.wait_ge(y_hi, k + 1)
                    pe.wait_ge(y_lo, k + 1)
                    down_unit(u, u % SLOTS, xhi, xlo, 2 * k, k == 0, order=NATURAL if k == 3 else None,
                              between={3: first_transposes(5)} if k == 3 else None)

            pe.wait_ge(ident_loaded, 16)
            first_transposes(0)()
            ffn(0)
            conv()
            ffn(1)
            ffn(2)
            gla()
            ffn(3)

        @block.scalar
        def _(act):
            def convert(u):
                if u >= UNITS:
                    return
                slot = u % SLOTS
                if u >= SLOTS:
                    act.wait_ge(unit_used, u - SLOTS + 1)
                act.wait_ge(raw_landed[slot], 16 * (u // SLOTS + 1))
                nc.scalar.copy(whi[:, slot, :], raw[:, slot, :]).then_inc(hi_made, 1)

            def convert_in_loop(u0, n, k):
                slot = (u0 + k) % SLOTS
                act.wait_ge(unit_used, u0 + 3 * n + k - SLOTS + 1)
                act.wait_ge(raw_landed[slot], 16 * ((u0 + k) // SLOTS + 1) + 16 * n)
                nc.scalar.copy(whi[:, slot, :], raw[:, slot, :]).then_inc(hi_made, 1)

            def norm_in(phase):
                for kt in range(KT):
                    act.wait_ge(x_trans, KT * phase + kt + 1)
                    at = (kt // 2) % 2 * SEQ
                    nc.scalar.activation(xhi[:, kt, :], ps[:, TR + kt % 2, at:at + SEQ], ACT.Copy,
                                         scale=chan_sb[:, C_NORM + phase * KT + kt:C_NORM + phase * KT + kt + 1]
                                         ).then_inc(x_hi, 1)
                    if phase == 0:
                        for k in {1: [0], 2: [1], 3: [2, 3]}.get(kt, []):
                            first_piece(k)
                        if kt == 4:
                            convert(1)
                        if kt == 7:
                            convert(2)
                    elif kt == 3:
                        convert(START[phase] + 2)
                    if kt == 5:
                        row_squares(phase, 0)
                row_squares(phase, 1)

            def first_piece(k):
                c = slice(k * 512, k * 512 + 512)
                act.wait_ge(pieces[k], 16)
                nc.scalar.copy(whi[:, 0, c], raw[:, 0, c]).then_inc(hi_piece, 1)
                if k == 3:
                    act.wait_ge(hi_piece, 4)
                    act.sem_inc(hi_made, 1)

            def row_squares(phase, t):
                if phase:
                    act.wait_ge(h_added, 4 * phase)
                if phase or t:
                    act.wait_ge(squares_done, TOKS * phase + t)
                nc.scalar.activation(squares[:, :], h[:, t, :], ACT.Square,
                                     accum_out=sumsq[:, t:t + 1]).then_inc(squares_done, 1)

            def ffn(f):
                phase, u0 = PHASE_OF_FFN[f], U_FFN[f]
                g0 = f * CHUNKS

                def silu(n):
                    done = u0 + 2 if isinstance(n, int) and n == 0 else u0 + 3 * n + 1
                    act.wait_ge(unit_used, done)
                    bank = DN if isinstance(n, int) and n == 0 else GU
                    for t in range(TOKS):
                        nc.scalar.activation(silu_g[:, t, :], ps[:, bank + t, 0:256], ACT.Silu,
                                             scale=rstd[:, t:t + 1]).then_inc(silu_done, 1)

                def high_of_gated(n, dst=ghi[:, :, :]):
                    act.wait_ge(g_trans, g0 + n + 1)
                    nc.scalar.copy(dst.rearrange("p a b -> p (a b)"), ps[:, TR, :]).then_inc(g_hi, 1)

                norm_in(phase)
                act.wait_ge(rstd_ready, phase + 1)
                convert(u0 + 3)
                silu(0)
                convert(u0 + 4)
                with act.Fori(1, CHUNKS - 1) as n:
                    high_of_gated(n - 1)
                    convert_in_loop(u0, n, 2)
                    silu(n)
                    convert_in_loop(u0, n, 3)
                    convert_in_loop(u0, n, 4)
                n = CHUNKS - 1
                high_of_gated(n - 1)
                convert(u0 + 3 * n + 2)
                silu(n)
                convert(u0 + 3 * n + 3)
                high_of_gated(n, xhi[:, KT - 2:KT, :])
                convert(u0 + 3 * n + 4)

            def conv():
                norm_in(1)
                act.wait_ge(const_made, 2)
                for c in range(CV_CHUNKS):
                    u = U_CONV + 2 * c
                    convert(u + 3)
                    if c >= 1:
                        channels_in(act, c - 1)
                    for t in range(TOKS):
                        act.wait_ge(cv_bias, 2 * c + t + 1)
                        nc.scalar.activation(sg[:, t, :], ag[:, t, 256:512], ACT.Sigmoid).then_inc(cv_sig, 1)
                    convert(u + 4)
                channels_in(act, CV_CHUNKS - 1)
                for i in range(DW_PE):
                    act.wait_ge(dw_pe, i + 1)
                    nc.scalar.activation(cvo[:, DW_DVE + i, :], ps[:, DW_BANKS[i], 0:SEQ], ACT.Identity,
                                         bias=chan_sb[:, C_BDW + DW_DVE + i:C_BDW + DW_DVE + i + 1]).then_inc(dw_out, 1)
                for j in range(4):
                    act.wait_ge(centred, j + 1)
                    nc.scalar.activation(cvs[:, 2 * j:2 * j + 2, :], cvo[:, 2 * j:2 * j + 2, :],
                                         ACT.Square).then_inc(cv_squares, 1)
                act.wait_ge(var_done, 1)
                nc.scalar.activation(ln_std, ps[:, 7, 0:SEQ], ACT.Sqrt, bias=eps_sb[:, 0:1]).then_inc(std_done, 1)
                for j in range(4):
                    act.wait_ge(normed, j + 1)
                    for ct in (2 * j, 2 * j + 1):
                        nc.scalar.activation(cvs[:, ct, :], cvo[:, ct, :], ACT.Silu,
                                             bias=chan_sb[:, C_LNB + ct:C_LNB + ct + 1],
                                             scale=chan_sb[:, C_LNG + ct:C_LNG + ct + 1]).then_inc(cv_act, 1)
                    act.wait_ge(cv_act, 2 * j + 2)
                    nc.scalar.copy(xhi[:, 2 * j:2 * j + 2, :], cvs[:, 2 * j:2 * j + 2, :]).then_inc(z_hi, 1)
                convert(U_CONV + 11)
                convert(U_CONV + 12)
                convert(U_CONV + 13)

            def channels_in(eng, c):
                eng.wait_ge(cv_trans, c + 1)
                if c == 0:
                    eng.wait_ge(hb_zero, 1)
                nc.scalar.copy(hb[:, 2 * c:2 * c + 2, PAD:PAD + SEQ],
                               ps[:, TR + c % 2, :].rearrange("p (a b) -> p a b", a=2)).then_inc(hb_ready, 1)

            def gla():
                U = U_GLA
                norm_in(4)
                act.wait_ge(rstd_ready, 5)
                convert(U + 3)

                def scaled(k, bank, dst, c0, signal):
                    act.wait_ge(unit_used, U + k + 1)
                    for t in range(TOKS):
                        nc.scalar.activation(dst[:, t, c0:c0 + 512], ps[:, bank + t, :], ACT.Copy,
                                             scale=rstd[:, t:t + 1]).then_inc(signal, 1)

                scaled(1, 0, q_tok, 0, qk_tok)
                act.wait_ge(za_done, 1)
                for t in range(TOKS):
                    nc.scalar.activation(za[:, t, :], ps[:, 4, t * 16:t * 16 + 16], ACT.Copy,
                                         scale=rstd[:, t:t + 1]).then_inc(za_scaled, 1)
                convert(U + 4)
                act.wait_ge(za_trans, 1)
                nc.scalar.copy(aT[0:16, :], ps[0:16, 5, 0:SEQ]).then_inc(aT_ready, 1)
                convert(U + 5)
                convert(U + 6)
                scaled(3, 2, k_tok, 0, qk_tok)
                act.wait_ge(zb_ready, HEADS)
                nc.scalar.activation(dif0, zb, ACT.Abs).then_inc(soft, 1)
                act.wait_ge(soft, 1)
                nc.scalar.activation(dif1, dif0, ACT.Exp, scale=-1.0).then_inc(soft, 1)
                act.wait_ge(soft, 2)
                nc.scalar.activation(dif0, dif1, ACT.Ln, bias=1.0).then_inc(soft, 1)
                for b in range(2):
                    act.wait_ge(qk_trans, b + 1)
                    nc.scalar.mul(qT[:, 2 * b:2 * b + 2, :], ps[:, TR + b, :].rearrange("p (a b) -> p a b", a=2),
                                  HK ** -0.5).then_inc(qkT_ready, 1)
                convert(U + 7)
                for b in range(2):
                    act.wait_ge(qk_trans, 2 + b + 1)
                    nc.scalar.copy(kT[:, 2 * b:2 * b + 2, :],
                                   ps[:, TR + b, :].rearrange("p (a b) -> p a b", a=2)).then_inc(qkT_ready, 1)
                convert(U + 8)

                def decay(lv):
                    act.wait_ge(dif_ready, 2 * (lv + 1))
                    nc.scalar.activation(dif[lv % 2], dif[lv % 2], ACT.Exp, scale=1.0 / TAU).then_inc(decay_ready, 1)

                def r_gate(c):
                    act.wait_ge(r_biased, 2 * (c + 1))
                    nc.scalar.activation(rg[:, :, c * 512:c * 512 + 512], rg[:, :, c * 512:c * 512 + 512],
                                         ACT.Silu).then_inc(r_silu, 1)

                decay(0)
                decay(1)
                convert(U + 9)
                decay(2)
                decay(3)
                convert(U + 10)
                decay(4)
                convert(U + 11)
                decay(5)
                convert(U + 12)
                scaled(9, 0, v_sb, 0, v_ready)
                decay(6)
                convert(U + 13)
                decay(7)
                convert(U + 14)
                scaled(11, 2, v_sb, 512, v_ready)
                r_gate(0)
                r_gate(1)
                act.wait_ge(scores, 2 * HEADS + 1)
                nc.scalar.copy(attn[:, :, :].rearrange("p (a b) c -> p a b c", b=3)[:, :, 2, :],
                               ps[:, 4, :].rearrange("p (a b) -> p a b", a=HEADS)).then_inc(attn_ready, 1)
                for hd in range(HEADS):
                    act.wait_ge(o_done, 2 * (hd // 2) + 2)
                    for t in range(TOKS):
                        if hd or t:
                            act.wait_ge(o_squares, 2 * hd + t)
                        nc.scalar.activation(masked[0][:, 0:2, :].rearrange("p a b -> p (a b)"),
                                             ps[:, 2 * t + hd // 2, (hd % 2) * HV:(hd % 2) * HV + HV], ACT.Square,
                                             accum_out=o_ss[:, 2 * hd + t:2 * hd + t + 1]).then_inc(o_squares, 1)
                for j in range(4):
                    act.wait_ge(y_trans, j + 1)
                    nc.scalar.copy(xhi[:, 2 * j:2 * j + 2, :],
                                   ps[:, TR + j % 2, :].rearrange("p (a b) -> p a b", a=2)).then_inc(y_hi, 1)
                convert(U + 15)
                convert(U + 16)
                convert(U + 17)

            START = [U_FFN[0], U_CONV, U_FFN[1], U_FFN[2], U_GLA, U_FFN[3]]
            act.dma_start(ident[:, :], ident_d).then_inc(ident_loaded, 16)
            act.dma_start(chan_sb[:, :], chan).then_inc(chan_loaded, 16)
            act.wait_ge(chan_loaded, 16)
            ffn(0)
            conv()
            ffn(1)
            act.wait_ge(z_lo, 4)
            act.dma_start(mask_sb.rearrange("p a b -> p (a b)"), masks).then_inc(gla_loaded, 16)
            act.dma_start(a1_raw, a1).then_inc(gla_loaded, 16)
            act.dma_start(a2_sb, a2).then_inc(gla_loaded, 16)
            ffn(2)
            gla()
            ffn(3)
            row_squares(6, 0)
            row_squares(6, 1)

        @block.vector
        def _(dve):
            def low(slot):
                nc.vector.tensor_tensor(wlo[:, slot, :], raw[:, slot, :], whi[:, slot, :].bitcast(F32),
                                        ALU.subtract).then_inc(lo_made, 1)

            def convert(u):
                if u >= UNITS:
                    return
                dve.wait_ge(hi_made, u + 1)
                if u - 1 in POOL_UNITS:
                    dve.wait_ge(lo_made, u)
                low(u % SLOTS)

            def convert_in_loop(u0, n, k):
                dve.wait_ge(hi_made, u0 + 3 * n + k + 1)
                low((u0 + k) % SLOTS)

            def norm_low(phase, kts):
                for kt in kts:
                    dve.wait_ge(x_hi, KT * phase + kt + 1)
                    at = (kt // 2) % 2 * SEQ
                    nc.vector.scalar_tensor_tensor(
                        out=xlo[:, kt, :], in0=ps[:, TR + kt % 2, at:at + SEQ],
                        scalar=chan_sb[:, C_NORM + phase * KT + kt:C_NORM + phase * KT + kt + 1],
                        in1=xhi[:, kt, :].bitcast(F32), op0=ALU.mult, op1=ALU.subtract).then_inc(x_lo, 1)

            def residual(phase, factor, last_unit):
                for n, (half, t) in enumerate(((0, 0), (1, 0), (0, 1), (1, 1)) if phase == 5
                                              else ((0, 0), (0, 1), (1, 0), (1, 1))):
                    if n < 3:
                        dve.wait_ge(down_part, 3 * phase + n + 1)
                    else:
                        if phase < 5:
                            norm_low(phase + 1, (0, 1))
                        dve.wait_ge(unit_used, last_unit + 1)
                    c = slice(half * 512, half * 512 + 512)
                    nc.vector.scalar_tensor_tensor(out=h[:, t, c], in0=ps[:, DN + 2 * t + half, :], scalar=factor,
                                                   in1=h[:, t, c], op0=ALU.mult, op1=ALU.add).then_inc(h_added, 1)

            def norm_in(phase):
                if phase == 0:
                    for kt in range(KT):
                        norm_low(0, (kt,))
                        for k in {1: [0], 2: [1], 3: [2, 3]}.get(kt, []):
                            first_piece(k)
                        if kt == 4:
                            convert(1)
                    convert(2)
                else:
                    norm_low(phase, range(2, 6))
                    convert(START[phase] + 2)
                    norm_low(phase, (6, 7))

            def first_piece(k):
                c = slice(k * 512, k * 512 + 512)
                dve.wait_ge(hi_piece, k + 1)
                nc.vector.tensor_tensor(wlo[:, 0, c], raw[:, 0, c], whi[:, 0, c].bitcast(F32),
                                        ALU.subtract).then_inc(lo_piece, 1)
                if k == 3:
                    dve.wait_ge(lo_piece, 4)
                    dve.sem_inc(lo_made, 1)

            def ffn(f):
                phase, u0 = PHASE_OF_FFN[f], U_FFN[f]
                g0 = f * CHUNKS

                def gate(n):
                    bank = DN if isinstance(n, int) and n == 0 else GU
                    for t in range(TOKS):
                        dve.wait_ge(silu_done, 2 * (g0 + n) + t + 1)
                        nc.vector.scalar_tensor_tensor(out=gated[:, t, :], in0=ps[:, bank + t, 256:512],
                                                       scalar=rstd[:, t:t + 1], in1=silu_g[:, t, :],
                                                       op0=ALU.mult, op1=ALU.mult).then_inc(gated_done, 1)

                def low_of_gated(n, dst=glo[:, :, :], high=ghi[:, :, :]):
                    dve.wait_ge(g_hi, g0 + n + 1)
                    nc.vector.tensor_tensor(dst.rearrange("p a b -> p (a b)"), ps[:, TR, :],
                                            high.rearrange("p a b -> p (a b)").bitcast(F32),
                                            ALU.subtract).then_inc(g_lo, 1)

                norm_in(phase)
                convert(u0 + 3)
                gate(0)
                convert(u0 + 4)
                with dve.Fori(1, CHUNKS - 1) as n:
                    low_of_gated(n - 1)
                    convert_in_loop(u0, n, 2)
                    gate(n)
                    convert_in_loop(u0, n, 3)
                    convert_in_loop(u0, n, 4)
                n = CHUNKS - 1
                low_of_gated(n - 1)
                convert(u0 + 3 * n + 2)
                gate(n)
                convert(u0 + 3 * n + 3)
                low_of_gated(n, xlo[:, KT - 2:KT, :], xhi[:, KT - 2:KT, :])
                residual(phase, 0.5, u0 + FFN_UNITS - 1)

            def conv():
                norm_in(1)
                dve.wait_ge(rstd_ready, 2)
                dve.wait_ge(bias_loaded, 32)

                def first_taps(ct0, n):
                    for ct in range(ct0, ct0 + n):
                        dve.wait_ge(hb_ready, ct // 2 + 1)
                        nc.vector.tensor_scalar(cvo[:, ct, :], hb[:, ct, 0:SEQ],
                                                chan_sb[:, C_DW + ct * TAPS:C_DW + ct * TAPS + 1],
                                                chan_sb[:, C_BDW + ct:C_BDW + ct + 1],
                                                ALU.mult, ALU.add).then_inc(dw_step, 1)

                def taps(run):
                    ct0, n, a, b = DW_RUNS[run]
                    base = dw_before(run) - n * a
                    with dve.Fori(a, b) as j:
                        for i in range(n):
                            ct = ct0 + i
                            dve.wait_ge(dw_step, n * j + (base - n + i + 1))
                            nc.vector.scalar_tensor_tensor(
                                out=cvo[:, ct, :], in0=hb[:, ct, bass.ds(j, SEQ)],
                                scalar=chan_sb[:, bass.ds(j + (C_DW + ct * TAPS), 1)],
                                in1=cvo[:, ct, :], op0=ALU.mult, op1=ALU.add).then_inc(dw_step, 1)

                for c in range(CV_CHUNKS):
                    u = U_CONV + 2 * c
                    if c == 1:
                        first_taps(0, 2)
                    if c:
                        taps(c - 1)
                    dve.wait_ge(unit_used, u + 2)
                    for t in range(TOKS):
                        if c:
                            dve.wait_ge(cv_gated, 2 * (c - 1) + t + 1)
                        nc.vector.scalar_tensor_tensor(out=ag[:, t, :], in0=ps[:, 2 * (c % 2) + t, :],
                                                       scalar=rstd[:, t:t + 1], in1=cvb[:, c * 512:c * 512 + 512],
                                                       op0=ALU.mult, op1=ALU.add).then_inc(cv_bias, 1)
                    if c:
                        dve.wait_ge(cv_trans, c)
                    for t in range(TOKS):
                        dve.wait_ge(cv_sig, 2 * c + t + 1)
                        nc.vector.tensor_tensor(gated[:, t, :], ag[:, t, 0:256], sg[:, t, :],
                                                ALU.mult).then_inc(cv_gated, 1)
                taps(3)
                first_taps(2, DW_DVE - 2)
                taps(4)
                dve.wait_ge(mean_done, 1)
                for j in range(4):
                    nc.vector.tensor_tensor(cvo[:, 2 * j:2 * j + 2, :], cvo[:, 2 * j:2 * j + 2, :],
                                            ps[:, 6, 0:SEQ].unsqueeze(1).to_broadcast([P, 2, SEQ]),
                                            ALU.subtract).then_inc(centred, 1)
                dve.wait_ge(std_done, 1)
                nc.vector.reciprocal(ln_rstd, ln_std).then_inc(ln_rstd_done, 1)
                dve.wait_ge(ln_rstd_done, 1)
                for j in range(4):
                    nc.vector.tensor_tensor(cvo[:, 2 * j:2 * j + 2, :], cvo[:, 2 * j:2 * j + 2, :],
                                            ln_rstd.unsqueeze(1).to_broadcast([P, 2, SEQ]),
                                            ALU.mult).then_inc(normed, 1)
                for j in range(4):
                    dve.wait_ge(z_hi, j + 1)
                    nc.vector.tensor_tensor(xlo[:, 2 * j:2 * j + 2, :], cvs[:, 2 * j:2 * j + 2, :],
                                            xhi[:, 2 * j:2 * j + 2, :].bitcast(F32), ALU.subtract).then_inc(z_lo, 1)
                convert(U_CONV + 11)
                convert(U_CONV + 12)
                dve.wait_ge(bias_added, 1)
                residual(1, 1.0, U_CONV + CV_UNITS - 1)

            def gla():
                U = U_GLA
                norm_in(4)
                convert(U + 3)
                convert(U + 4)
                convert(U + 5)
                convert(U + 6)
                dve.wait_ge(a2_done, 1)
                for hd in range(HEADS):
                    nc.vector.tensor_scalar(zb[:, hd, :], ps[:, 4 + hd // 2, (hd % 2) * SEQ:(hd % 2) * SEQ + SEQ],
                                            chan_sb[:, C_BA + hd:C_BA + hd + 1], None, ALU.add).then_inc(zb_ready, 1)
                dve.wait_ge(soft, 3)
                nc.vector.scalar_tensor_tensor(out=zb, in0=zb, scalar=0.0, in1=dif0,
                                               op0=ALU.min, op1=ALU.subtract).then_inc(la_ready, 1)
                dve.wait_ge(keep_ready, 3)
                dve.wait_ge(la_ready, 1)
                for hd in range(HEADS):
                    nc.vector.tensor_tensor_scan(b64[:, hd, :], keep64, zb[:, hd, :], 0.0,
                                                 ALU.mult, ALU.add).then_inc(scanned, 1)
                    nc.vector.tensor_tensor_scan(b256[:, hd, :], keep_all, zb[:, hd, :], 0.0,
                                                 ALU.mult, ALU.add).then_inc(scanned, 1)
                convert(U + 7)
                convert(U + 8)
                dve.wait_ge(scanned, 2 * HEADS)
                dve.wait_ge(rstd_ready, 5)

                def difference(lv):
                    m = 2 ** lv
                    b = b64 if m <= 32 else b256
                    bv = b.rearrange("p a b -> p (a b)").rearrange("p (g two m) -> p g two m", two=2, m=m)
                    dv = dif[lv % 2].rearrange("p a b -> p (a b)").rearrange("p (g two m) -> p g two m", two=2, m=m)
                    groups = HEADS * SEQ // (2 * m)
                    mid = bv[:, :, 0, m - 1:m].to_broadcast([P, groups, m])
                    if lv >= 2:
                        dve.wait_ge(qk_ready, 2 * (lv - 1))
                    nc.vector.tensor_tensor(dv[:, :, 0, :], mid, bv[:, :, 0, :], ALU.subtract).then_inc(dif_ready, 1)
                    nc.vector.tensor_tensor(dv[:, :, 1, :], bv[:, :, 1, :], mid, ALU.subtract).then_inc(dif_ready, 1)

                def r_bias(c):
                    dve.wait_ge(unit_used, U + 5 + 2 * c + 1)
                    for t in range(TOKS):
                        nc.vector.scalar_tensor_tensor(out=rg[:, t, c * 512:c * 512 + 512], in0=ps[:, 2 * c + t, :],
                                                       scalar=rstd[:, t:t + 1], in1=rows_sb[:, c * 512:c * 512 + 512],
                                                       op0=ALU.mult, op1=ALU.add).then_inc(r_biased, 1)

                difference(0)
                difference(1)
                convert(U + 9)
                r_bias(0)
                difference(2)
                difference(3)
                convert(U + 10)
                difference(4)
                r_bias(1)
                convert(U + 11)
                difference(5)
                convert(U + 12)
                difference(6)
                convert(U + 13)
                difference(7)
                convert(U + 14)
                dve.wait_ge(gla_loaded, 48)
                for i in range(2 * HEADS):
                    hd, tile = i // 2, i % 2
                    bank = 4 + 2 * (i % 2)
                    dve.wait_ge(scores, i + 1)
                    if i >= 2:
                        dve.wait_ge(attn_ready, i - 1)
                    mk = masked[i % 2]
                    nc.vector.tensor_tensor(mk, ps[:, bank:bank + 2, :].rearrange("p a (l t) -> p (a l) t", t=P),
                                            mask_sb[:, :, :], ALU.mult).then_inc(masked_ready, 1)
                    dve.wait_ge(masked_ready, i + 1)
                    if i == 0:
                        dve.wait_ge(qk_ready, 2 * LEVELS)
                    nc.vector.tensor_reduce(attn[:, 3 * hd + tile, :], mk.rearrange("p l t -> p t l"),
                                            AX_X, ALU.add).then_inc(attn_ready, 1)
                dve.wait_ge(o_rstd_done, 1)
                dve.wait_ge(rg_ready, 2)
                for hd in range(HEADS):
                    for t in range(TOKS):
                        c = slice(hd * HV, hd * HV + HV)
                        nc.vector.scalar_tensor_tensor(
                            out=y_tok[:, t, c], in0=ps[:, 2 * t + hd // 2, (hd % 2) * HV:(hd % 2) * HV + HV],
                            scalar=o_rstd[:, 2 * hd + t:2 * hd + t + 1], in1=rg[:, t, c],
                            op0=ALU.mult, op1=ALU.mult).then_inc(y_ready, 1)
                for j in range(4):
                    dve.wait_ge(y_hi, j + 1)
                    nc.vector.tensor_tensor(xlo[:, 2 * j:2 * j + 2, :],
                                            ps[:, TR + j % 2, :].rearrange("p (a b) -> p a b", a=2),
                                            xhi[:, 2 * j:2 * j + 2, :].bitcast(F32), ALU.subtract).then_inc(y_lo, 1)
                convert(U + 15)
                convert(U + 16)
                residual(4, 1.0, U + GLA_UNITS - 1)

            START = [U_FFN[0], U_CONV, U_FFN[1], U_FFN[2], U_GLA, U_FFN[3]]
            dve.wait_ge(chan_loaded, 16)
            ffn(0)
            conv()
            ffn(1)
            ffn(2)
            gla()
            ffn(3)
            dve.wait_ge(rstd_ready, 7)
            dve.wait_ge(gain_loaded, 16)
            for t in range(TOKS):
                nc.vector.scalar_tensor_tensor(out=h[:, t, :], in0=h[:, t, :], scalar=rstd[:, t:t + 1],
                                               in1=pair[:, :], op0=ALU.mult, op1=ALU.mult).then_inc(out_ready, 1)

        @block.gpsimd
        def _(pool):
            nc.gpsimd.memset(mean_w[:, :], 1.0 / D).then_inc(const_made, 1)
            nc.gpsimd.memset(eps_sb[:, :], EPS).then_inc(const_made, 1)
            nc.gpsimd.memset(neg_half[:, :], -0.5).then_inc(const_made, 1)
            nc.gpsimd.memset(hb[:, :, 0:PAD], 0.0).then_inc(hb_zero, 1)

            def row_rstd(phase):
                pool.wait_ge(squares_done, TOKS * (phase + 1))
                nc.gpsimd.tensor_scalar(ms[:, :], sumsq[:, :], 1.0 / D, EPS, ALU.mult, ALU.add).then_inc(ms_done, 1)
                pool.wait_ge(ms_done, phase + 1)
                nc.gpsimd.tensor_tensor(rstd[:, :], ms[:, :], neg_half[:, 0:TOKS], ALU.pow).then_inc(rstd_ready, 1)

            def low(u):
                slot = u % SLOTS
                pool.wait_ge(hi_made, u + 1)
                pool.wait_ge(lo_made, u)
                nc.gpsimd.tensor_tensor(wlo[:, slot, :], raw[:, slot, :], whi[:, slot, :].bitcast(F32),
                                        ALU.subtract).then_inc(lo_made, 1)

            pool.wait_ge(const_made, 3)
            row_rstd(0)
            pool.wait_ge(ident_loaded, 16)
            pool.wait_ge(chan_loaded, 16)
            for i in range(DW_PE):
                ct = DW_DVE + i
                nc.gpsimd.tensor_tensor(diag[:, i, :, :], ident[:, :].unsqueeze(1).to_broadcast([P, TAPS, P]),
                                        chan_sb[:, C_DW + ct * TAPS:C_DW + (ct + 1) * TAPS].unsqueeze(2)
                                        .to_broadcast([P, TAPS, P]), ALU.mult).then_inc(diag_made, 1)
            low(U_CONV + 1)
            row_rstd(1)
            pool.wait_ge(bias_loaded, 32)
            for u in range(U_CONV + 3, U_CONV + 11):
                low(u)
                if u == U_CONV + 5:
                    pool.wait_ge(x_trans, 2 * KT)
                    nc.gpsimd.tensor_tensor(h[:, :, :], h[:, :, :],
                                            cvb[:, 2 * D:3 * D].unsqueeze(1).to_broadcast([P, TOKS, D]),
                                            ALU.add).then_inc(bias_added, 1)
            low(U_FFN[1] + 1)
            row_rstd(2)
            low(U_FFN[2] + 1)
            row_rstd(3)
            pool.wait_ge(gla_loaded, 48)
            nc.gpsimd.tensor_copy(a1_hi[:, :], a1_raw).then_inc(a1_split, 1)
            pool.wait_ge(a1_split, 1)
            nc.gpsimd.tensor_tensor(a1_lo[:, :], a1_raw, a1_hi[:, :].bitcast(F32),
                                    ALU.subtract).then_inc(a1_split, 1)
            low(U_GLA + 1)
            row_rstd(4)
            nc.gpsimd.memset(keep64, 1.0).then_inc(keep_ready, 1)
            nc.gpsimd.memset(keep_all, 1.0).then_inc(keep_ready, 1)
            pool.wait_ge(keep_ready, 1)
            nc.gpsimd.memset(keep64.rearrange("p (c t) -> p c t", t=64)[:, :, 0:1], 0.0).then_inc(keep_ready, 1)
            for lv in range(LEVELS):
                m = 2 ** lv
                pool.wait_ge(decay_ready, lv + 1)
                if lv == 0:
                    pool.wait_ge(qkT_ready, 4)
                split = "p (g two m) -> p g two m"
                dv = dif[lv % 2].rearrange("p a b -> p (a b)").rearrange(split, two=2, m=m)
                ov = qk[:, lv, :].rearrange(split, two=2, m=m)
                for part, src in ((0, kT), (1, qT)):
                    sv = src.rearrange("p a b -> p (a b)").rearrange(split, two=2, m=m)
                    nc.gpsimd.tensor_tensor(ov[:, :, part, :], dv[:, :, part, :], sv[:, :, part, :],
                                            ALU.mult).then_inc(qk_ready, 1)
            for c in range(2):
                pool.wait_ge(r_silu, c + 1)
                for t in range(TOKS):
                    rv = rg[:, t, c * 512:c * 512 + 512].rearrange("p (a b) -> p a b", b=HV)
                    ins = nc.gpsimd.tensor_tensor(rv, rv, rows_sb[:, D:D + HV].unsqueeze(1)
                                                  .to_broadcast([P, 2, HV]), ALU.mult)
                ins.then_inc(rg_ready, 1)
            pool.wait_ge(o_squares, 2 * HEADS)
            nc.gpsimd.tensor_scalar(o_ms, o_ss, 1.0 / HV, EPS, ALU.mult, ALU.add).then_inc(o_ms_done, 1)
            pool.wait_ge(o_ms_done, 1)
            nc.gpsimd.tensor_tensor(o_rstd, o_ms, neg_half[:, :], ALU.pow).then_inc(o_rstd_done, 1)
            low(U_FFN[3] + 1)
            row_rstd(5)
            row_rstd(6)


INS = ["stream", "x", "chan", "rows", "a1", "a2", "masks", "ident"]


def level_masks():
    s, t = np.arange(P)[:, None], np.arange(P)[None, :]
    out = [s == t]
    for lv in range(LEVELS - 1):
        m = 2 ** lv
        out.append((s // (2 * m) == t // (2 * m)) & (s // m % 2 == 0) & (t // m % 2 == 1))
    return np.stack(out, axis=1).astype(np.float32).reshape(P, LEVELS * P)


def kernel(**inputs):
    import concourse.bacc as _bacc
    from concourse.bass_utils import run_bass_kernel_spmd as _run

    a = {k: np.asarray(v) for k, v in inputs.items()}

    def wide(left, right, chunk):
        n = left.shape[1] // chunk
        both = [w.reshape(2, 4, P, n, chunk) for w in (left, right)]
        both = np.concatenate(both, axis=4)
        return both.transpose(3, 0, 2, 1, 4).reshape(2 * n, P, UNIT)

    def single(w):
        return w.reshape(2, 4, P, w.shape[1] // 512, 512).transpose(3, 0, 2, 1, 4).reshape(-1, P, UNIT)

    def down(w):
        return w.reshape(-1, 2, P, D).transpose(0, 2, 1, 3).reshape(-1, P, UNIT)

    def ffn(name, i):
        gu = wide(a[name + "_gate"][i], a[name + "_up"][i], 256).reshape(CHUNKS, 2, P, UNIT)
        dn = down(a[name + "_down"][i])
        parts = [gu[0]]
        for n in range(1, CHUNKS):
            parts += [gu[n], dn[n - 1:n]]
        return np.concatenate(parts + [dn[CHUNKS - 1:]])

    pw1 = a["cv_w_pw1"][0]
    stream = np.concatenate([
        ffn("w1", 0), wide(pw1[:, :D], pw1[:, D:], 256), down(a["cv_w_pw2"][0]), ffn("w2", 0), ffn("w1", 1),
        single(a["gla_w_q"][0]), single(a["gla_w_k"][0]), single(a["gla_w_r"][0]), single(a["gla_w_v"][0]),
        down(a["gla_w_o"][0]), ffn("w2", 1)])

    def col(v):
        return v.reshape(-1, P).T

    norms = [a["g_ffn1"][0], a["g_mix"][0], a["g_ffn2"][0], a["g_ffn1"][1], a["g_mix"][1], a["g_ffn2"][1]]
    dw = a["cv_w_dw"][0].reshape(TAPS, KT, P).transpose(2, 1, 0).reshape(P, KT * TAPS)
    chan = np.concatenate([col(v) for v in norms] + [dw, col(a["cv_b_dw"][0]), col(a["cv_ln_g"][0]),
                                                     col(a["cv_ln_b"][0]), col(a["gla_b_a"][0])], axis=1)
    bpw1 = a["cv_b_pw1"][0].reshape(2, CV_CHUNKS, 256).transpose(1, 0, 2).reshape(-1)
    rows = np.concatenate([bpw1, a["cv_b_pw2"][0], a["gla_b_r"][0], a["gla_norm_g"][0], a["g_final"]])
    arrays = {
        "stream": stream, "x": a["x"], "chan": chan, "rows": rows,
        "a1": a["gla_w_a1"][0].reshape(KT, P, 16).transpose(1, 0, 2).reshape(P, KT * 16),
        "a2": a["gla_w_a2"][0], "masks": level_masks(), "ident": np.eye(P, dtype=np.float32),
    }
    arrays = {f"in_{k}_dram": np.ascontiguousarray(v) for k, v in arrays.items()}
    nc = _bacc.Bacc("TRN2", target_bir_lowering=False, num_devices=1)
    args = [nc.dram_tensor(f"in_{k}_dram", arrays[f"in_{k}_dram"].shape, mybir.dt.float32, kind="ExternalInput").ap()
            for k in INS]
    out = nc.dram_tensor("out_0_dram", (1, SEQ, D), mybir.dt.float32, kind="ExternalOutput").ap()
    build(nc, *args, out)
    r = _run(nc, [arrays], core_ids=[0])
    return r.results[0]["out_0_dram"]
```

```python
from contextlib import ExitStack

import numpy as np

import concourse.bass as bass
from concourse import mybir
from concourse.alu_op_type import AluOpType as ALU

F32 = mybir.dt.float32
F32R = mybir.dt.float32r
ACT = mybir.ActivationFunctionType
AX_X = mybir.AxisListType.X

P = 128
D = 1024
SEQ = 256
FF = 2816
TOKS = SEQ // P
KT = D // P
EPS = 1e-6
UNIT = 2048
SLOTS = 3
CHUNKS = FF // 256
FFN_UNITS = 3 * CHUNKS
TAPS = 31
PAD = TAPS - 1
CV_CHUNKS = D // 256
CV_UNITS = 2 * CV_CHUNKS + 4
HEADS = 4
HK = 128
HV = 256
TAU = 16.0
LEVELS = 8
GLA_UNITS = 16

U_FFN = [0, FFN_UNITS + CV_UNITS, 2 * FFN_UNITS + CV_UNITS, 3 * FFN_UNITS + CV_UNITS + GLA_UNITS]
U_CONV = FFN_UNITS
U_GLA = 3 * FFN_UNITS + CV_UNITS
UNITS = U_FFN[3] + FFN_UNITS
PHASE_OF_FFN = [0, 2, 3, 5]

DW_DVE = 4
DW_SIDE = DW_DVE
DW_PE = KT - DW_DVE - 1
DW_SHARED = 9
SIDE_TAPS = 5

C_NORM = 0
C_DW = C_NORM + 6 * KT
C_BDW = C_DW + KT * TAPS
C_LNG = C_BDW + KT
C_LNB = C_LNG + KT
C_BA = C_LNB + KT
C_NG = C_BA + HEADS
C_END = C_NG + HV // P
R_BPW1 = 0
R_BPW2 = R_BPW1 + 2 * D
R_BR = R_BPW2 + D
R_GF = R_BR + D
R_END = R_GF + D
MASKS = LEVELS - 1


def build(nc, stream, x, chan, rows, a1, a2, masks, ident_d, out):
    with ExitStack() as ctx:
        def sb(name, shape, dt=F32):
            return ctx.enter_context(nc.sbuf_tensor(name, shape, dt))

        def sem(name):
            return ctx.enter_context(nc.semaphore(name))

        ps = ctx.enter_context(nc.psum_tensor("ps", [P, 8, 512], F32))
        GU, DN, TR = 0, 2, 6
        DW_BANKS = [4, 5, 0]

        h = sb("h", [P, TOKS, D])
        raw = sb("raw", [P, SLOTS, UNIT])
        whi = sb("whi", [P, SLOTS, UNIT], F32R)
        wlo = sb("wlo", [P, SLOTS, UNIT], F32R)
        xhi = sb("xhi", [P, KT, SEQ], F32R)
        xlo = sb("xlo", [P, KT, SEQ], F32R)
        ghi = sb("ghi", [P, 2, SEQ], F32R)
        glo = sb("glo", [P, 2, SEQ], F32R)
        pair = sb("pair", [P, D])
        silu_g = pair[:, 0:512].rearrange("p (t c) -> p t c", t=TOKS)
        gated = pair[:, 512:1024].rearrange("p (t c) -> p t c", t=TOKS)
        squares = sb("squares", [P, D])
        chan_sb = sb("chan_sb", [P, C_END])
        rows_sb = sb("rows_sb", [P, R_GF - R_BR])
        ident = sb("ident", [P, P])
        a1_hi = sb("a1_hi", [P, KT * 16], F32R)
        a1_lo = sb("a1_lo", [P, KT * 16], F32R)
        mean_w = sb("mean_w", [P, P])
        mean_sq = sb("mean_sq", [P, TOKS])
        rstd = sb("rstd", [P, TOKS])
        ms = sb("ms", [P, TOKS])
        half_sq = sb("half_sq", [P, 2 * TOKS])
        neg_half = sb("neg_half", [P, TOKS])
        WORK = 22912
        work = sb("work", [P, WORK])

        def area(at, *shape):
            n = int(np.prod(shape))
            v = work[:, at:at + n]
            assert at + n <= WORK, (at, n)
            if len(shape) == 2:
                v = v.rearrange("p (a b) -> p a b", a=shape[0])
            if len(shape) == 3:
                v = v.rearrange("p (a b c) -> p a b c", a=shape[0], b=shape[1])
            return v, at + n

        diag, at = area(0, DW_PE, TAPS, P)
        hb, at = area(at, KT, PAD + SEQ)
        cvo, at = area(at, KT, SEQ)
        cvs, at = area(at, KT, SEQ)
        ln_at = at
        ag, at = area(at, TOKS, 512)
        sg, at = area(at, TOKS, 256)
        ln_diag, ln_at = area(ln_at, TOKS, P)
        ln_var, ln_at = area(ln_at, TOKS)
        ln_rstd, _ = area(ln_at, TOKS)
        cvb, at = area(at, R_BR)
        q_tok = squares[:, :].rearrange("p (t c) -> p t c", t=TOKS)
        k_tok = pair[:, :].rearrange("p (t c) -> p t c", t=TOKS)
        qT, at = area(0, HEADS, SEQ)
        kT, at = area(at, HEADS, SEQ)
        v_sb, at = area(at, TOKS, D)
        rg, at = area(at, TOKS, D)
        y_at = at
        zb, at = area(at, HEADS, SEQ)
        dif0, at = area(at, HEADS, SEQ)
        dif1, at = area(at, HEADS, SEQ)
        b64, at = area(at, HEADS, SEQ)
        b256, at = area(at, HEADS, SEQ)
        qk, at = area(at, LEVELS, HEADS * SEQ)
        keep64, at = area(at, SEQ)
        keep_all, at = area(at, SEQ)
        za, at = area(at, SEQ)
        aT, at = area(at, SEQ)
        o_ms, at = area(at, 8)
        o_me, at = area(at, 8)
        o_rstd, at = area(at, 8)
        mask_sb, at = area(at, MASKS, P)
        a1_raw, at = area(at, KT * 16)
        a2_sb, at = area(at, HEADS * HK)
        a2_sb = a2_sb[0:16, :]
        rstd_diag = dif1[:, 0, :].rearrange("p (t c) -> p t c", t=TOKS)
        dif = [dif0, dif1, zb]
        masked = [squares[:, :].rearrange("p (l t) -> p l t", l=LEVELS),
                  pair[:, :].rearrange("p (l t) -> p l t", l=LEVELS)]
        y_tok, at2 = area(y_at, TOKS, D)
        attn, at2 = area(at2, HEADS * 3, P)
        o_sq = b256[:, 0, :]

        x_loaded = [[sem(f"x_loaded{t}_{half}") for half in range(2)] for t in range(TOKS)]
        ident_loaded = sem("ident_loaded")
        chan_loaded = sem("chan_loaded")
        gla_loaded = sem("gla_loaded")
        piece_landed = [sem(f"piece_landed{k}") for k in range(4 * SLOTS)]
        hi_piece = sem("hi_piece")
        lo_piece = sem("lo_piece")
        bias_loaded = sem("bias_loaded")
        gain_loaded = sem("gain_loaded")
        raw_landed = [sem(f"raw_landed{s}") for s in range(SLOTS)]
        hi_made = sem("hi_made")
        lo_made = sem("lo_made")
        unit_used = sem("unit_used")
        h_added = sem("h_added")
        x_trans = sem("x_trans")
        x_hi = sem("x_hi")
        x_lo = sem("x_lo")
        squares_done = sem("squares_done")
        ms_done = sem("ms_done")
        rstd_ready = sem("rstd_ready")
        o_eps_added = sem("o_eps_added")
        silu_done = sem("silu_done")
        gated_done = sem("gated_done")
        g_trans = sem("g_trans")
        g_hi = sem("g_hi")
        g_lo = sem("g_lo")
        down_part = sem("down_part")
        const_made = sem("const_made")
        diag_made = sem("diag_made")
        cv_bias = sem("cv_bias")
        cv_sig = sem("cv_sig")
        cv_gated = sem("cv_gated")
        cv_trans = sem("cv_trans")
        hb_zero = sem("hb_zero")
        hb_ready = sem("hb_ready")
        dw_step = sem("dw_step")
        side_product = sem("side_product")
        side_step = sem("side_step")
        dw_pe = sem("dw_pe")
        dw_out = sem("dw_out")
        mean_done = sem("mean_done")
        centred = sem("centred")
        cv_squares = sem("cv_squares")
        var_done = sem("var_done")
        ln_var_ready = sem("ln_var_ready")
        ln_pow_done = sem("ln_pow_done")
        ln_spread = sem("ln_spread")
        ln_rstd_done = sem("ln_rstd_done")
        normed = sem("normed")
        cv_act = sem("cv_act")
        z_hi = sem("z_hi")
        z_lo = sem("z_lo")
        bias_added = sem("bias_added")
        a1_split = sem("a1_split")
        za_done = sem("za_done")
        za_copied = sem("za_copied")
        norm_diag = sem("norm_diag")
        norm_spread = sem("norm_spread")
        aT_ready = sem("aT_ready")
        a2_done = sem("a2_done")
        zb_ready = sem("zb_ready")
        soft = sem("soft")
        la_ready = sem("la_ready")
        scanned = sem("scanned")
        keep_ready = sem("keep_ready")
        qk_tok = sem("qk_tok")
        k_scaled = sem("k_scaled")
        v_ready = sem("v_ready")
        r_biased = sem("r_biased")
        r_silu = sem("r_silu")
        qk_trans = sem("qk_trans")
        qkT_ready = sem("qkT_ready")
        dif_ready = sem("dif_ready")
        decay_ready = sem("decay_ready")
        qk_ready = sem("qk_ready")
        scores = sem("scores")
        masked_ready = sem("masked_ready")
        attn_ready = sem("attn_ready")
        cross_ready = sem("cross_ready")
        o_done = sem("o_done")
        o_squares = sem("o_squares")
        o_rstd_done = sem("o_rstd_done")
        y_ready = sem("y_ready")
        y_trans = sem("y_trans")
        y_hi = sem("y_hi")
        y_lo = sem("y_lo")
        out_ready = sem("out_ready")
        stored = sem("stored")

        POOL_UNITS = {U_CONV + 1, U_FFN[1] + 1, U_FFN[2] + 1, U_GLA + 1, U_FFN[3] + 1, *range(U_CONV + 3, U_CONV + 11),
                      *range(U_GLA + 11, U_GLA + 15)}

        DW_RUNS = [(0, 2, 1, 7, 3), (0, 2, 7, 16, 3), (0, 2, 16, TAPS, 5), (2, DW_DVE - 2, 1, TAPS, 5)]
        DW_STEPS = DW_DVE * TAPS

        def dw_before(run):
            steps = sum(n * (b - a) for _, n, a, b, _ in DW_RUNS[:run])
            return steps + (2 if run < 3 else DW_DVE)

        def dw_last(ct):
            run = 2 if ct < 2 else 3
            ct0, n, a, b, _ = DW_RUNS[run]
            return dw_before(run) + n * (b - a - 1) + ct - ct0 + 1

        QUARTERS_AFTER = {1: [0], 2: [1], 3: [2], 4: [3], 5: [4], 6: [5], 7: range(6, 12)}

        block = ctx.enter_context(nc.Block())

        @block.sync
        def _(sp):
            xv = x.rearrange("a (t p) d -> t p (a d)", p=P)

            def load_x(half):
                c = slice(half * 512, half * 512 + 512)
                for t in range(TOKS):
                    sp.dma_start(h[:, t, c], xv[t, :, c]).then_inc(x_loaded[t][half], 16)

            load_x(0)
            for k in range(4 * SLOTS):
                c = slice(k % 4 * 512, k % 4 * 512 + 512)
                sp.dma_start(raw[:, k // 4, c], stream[k // 4, :, c]).then_inc(piece_landed[k], 16)
                if k == 2:
                    load_x(1)

            def load(u, slot):
                sp.wait_ge(lo_made, u - SLOTS + 1)
                sp.dma_start(raw[:, slot, :], stream[bass.ds(u, 1), :, :]
                             .rearrange("a p n -> p (a n)")).then_inc(raw_landed[slot], 16)

            whole = UNITS // SLOTS
            for u in range(SLOTS, 2 * SLOTS):
                load(u, u % SLOTS)
            sp.dma_start(cvb, rows[0:R_BR].partition_broadcast(P)).then_inc(bias_loaded, 16)
            sp.dma_start(rows_sb[:, :], rows[R_BR:R_GF].partition_broadcast(P)).then_inc(bias_loaded, 16)
            with sp.Fori(2, whole) as turn:
                for slot in range(SLOTS):
                    load(turn * SLOTS + slot, slot)
            for u in range(whole * SLOTS, UNITS):
                load(u, u % SLOTS)
            sp.wait_ge(g_trans, 4 * CHUNKS)
            sp.dma_start(pair[:, :], rows[R_GF:R_END].partition_broadcast(P)).then_inc(gain_loaded, 16)
            for t in range(TOKS):
                for half in range(2):
                    c = slice(half * 512, half * 512 + 512)
                    sp.wait_ge(out_ready, 2 * t + half + 1)
                    sp.dma_start(out.rearrange("a (t p) d -> t p (a d)", p=P)[t, :, c], h[:, t, c]).then_inc(stored, 16)
            sp.wait_ge(stored, 2 * 16 * TOKS)

        @block.tensor
        def _(pe):
            def unit_ready(u):
                pe.wait_ge(hi_made, u + 1)
                pe.wait_ge(lo_made, u + 1)

            def in_quarters(u):
                return isinstance(u, int) and u < SLOTS

            def keep_busy(n):
                for _ in range(n):
                    nc.tensor.matmul(ps[:, 1, 0:P], mean_w[:, :], mean_w[:, :], start=True, stop=True)

            NATURAL = [(0, 0), (0, 1), (1, 0), (1, 1)]
            BY_TOKENS = [(0, 0), (1, 0), (0, 1), (1, 1)]

            def three(o, xh, xl, wh, wl, first, last):
                nc.tensor.matmul(o, xh, wh, start=first, stop=False)
                nc.tensor.matmul(o, xh, wl, start=False, stop=False)
                return nc.tensor.matmul(o, xl, wh, start=False, stop=last)

            def wide_unit(u, slot, half, bank, phase=None, between=None):
                if not in_quarters(u):
                    unit_ready(u)
                for k in range(4):
                    kt = 4 * half + k
                    if between and k in between:
                        between[k]()
                    if phase is not None:
                        pe.wait_ge(x_hi, KT * phase + kt + 1)
                        pe.wait_ge(x_lo, KT * phase + kt + 1)
                        if kt + 2 < KT:
                            norm_transpose(phase, kt + 2)
                    if in_quarters(u):
                        pe.wait_ge(hi_piece, 4 * u + k + 1)
                        pe.wait_ge(lo_piece, 4 * u + k + 1)
                    w = slice(k * 512, k * 512 + 512)
                    for t in range(TOKS):
                        s = slice(t * P, t * P + P)
                        last = three(ps[:, bank + t, :], xhi[:, kt, s], xlo[:, kt, s],
                                     whi[:, slot, w], wlo[:, slot, w], kt == 0, kt == KT - 1)
                last.then_inc(unit_used, 1)

            def down_unit(u, slot, srch, srcl, k0, first, order=NATURAL, final=False, between=None, inputs=None):
                unit_ready(u)
                for n, (half, t) in enumerate(order):
                    if between and n in between:
                        between[n]()
                    s = slice(t * P, t * P + P)
                    for k in range(2):
                        if inputs and n == 0:
                            inputs(k)
                        w = slice(k * D + half * 512, k * D + half * 512 + 512)
                        last = three(ps[:, DN + 2 * t + half, :], srch[:, k0 + k, s], srcl[:, k0 + k, s],
                                     whi[:, slot, w], wlo[:, slot, w], first and k == 0, final and k == 1)
                    if final and n < 3:
                        last.then_inc(down_part, 1)
                last.then_inc(unit_used, 1)

            def turn(bank, src, c0):
                for k in range(2):
                    for t in range(TOKS):
                        last = nc.tensor.transpose(ps[:, bank, k * SEQ + t * P:k * SEQ + t * P + P],
                                                   src[:, t, c0 + k * P:c0 + k * P + P], ident[:, :])
                return last

            def norm_transpose(phase, kt):
                if phase:
                    pe.wait_ge(h_added, 4 * (phase - 1) + 2 * (kt // 4 + 1))
                if kt >= 2:
                    pe.wait_ge(x_lo, KT * phase + kt - 1)
                for t in range(TOKS):
                    if phase == 0 and kt % 4 == 0:
                        pe.wait_ge(x_loaded[t][kt // 4], 16)
                    at = (kt // 2) % 2 * SEQ + t * P
                    last = nc.tensor.transpose(ps[:, TR + kt % 2, at:at + P], h[:, t, kt * P:kt * P + P], ident[:, :])
                last.then_inc(x_trans, 1)

            def first_transposes(phase):
                def do():
                    norm_transpose(phase, 0)
                    norm_transpose(phase, 1)
                return do

            def ffn(f):
                phase, u0, s0 = PHASE_OF_FFN[f], U_FFN[f], U_FFN[f] % SLOTS
                g0 = f * CHUNKS

                def chunk(n, first=False, last=False):
                    u = u0 + 3 * n - 1
                    if not first:
                        pe.wait_ge(gated_done, 2 * (g0 + n))
                    wide_unit(u, (s0 + 2) % SLOTS, 0, GU)
                    if first:
                        pe.wait_ge(gated_done, 2 * (g0 + n))
                    turn(TR, gated, 0).then_inc(g_trans, 1)
                    wide_unit(u + 1, s0, 1, GU)
                    pe.wait_ge(g_hi, g0 + n)
                    pe.wait_ge(g_lo, g0 + n)
                    down_unit(u + 2, (s0 + 1) % SLOTS, ghi, glo, 0, first, between={2: last_turn} if last else None)

                def last_turn():
                    pe.wait_ge(gated_done, 2 * (g0 + CHUNKS))
                    turn(TR, gated, 0).then_inc(g_trans, 1)

                if phase:
                    pe.wait_ge(h_added, 4 * (phase - 1) + 3)
                wide_unit(u0, s0, 0, DN, phase)
                wide_unit(u0 + 1, (s0 + 1) % SLOTS, 1, DN, phase)
                chunk(1, first=True)
                with pe.Fori(2, CHUNKS - 1) as n:
                    chunk(n)
                chunk(CHUNKS - 1, last=True)
                pe.wait_ge(g_hi, g0 + CHUNKS)
                pe.wait_ge(g_lo, g0 + CHUNKS)
                down_unit(u0 + FFN_UNITS - 1, (s0 + 2) % SLOTS, xhi, xlo, KT - 2, False,
                          order=BY_TOKENS if f == 3 else NATURAL, final=True,
                          between=None if f == 3 else {3: first_transposes(phase + 1)})

            def conv():
                for c in range(CV_CHUNKS):
                    u = U_CONV + 2 * c
                    bank = 2 * (c % 2)
                    if c >= 2:
                        pe.wait_ge(cv_bias, 2 * (c - 1))
                    if c == 1:
                        pe.wait_ge(h_added, 4)
                    wide_unit(u, u % SLOTS, 0, bank, 1 if c == 0 else None)
                    if c >= 1:
                        pe.wait_ge(cv_gated, 2 * c)
                        if c >= 3:
                            pe.wait_ge(hb_ready, c - 2)
                        turn(TR + (c - 1) % 2, gated, 0).then_inc(cv_trans, 1)
                    wide_unit(u + 1, (u + 1) % SLOTS, 1, bank, 1 if c == 0 else None)
                pe.wait_ge(diag_made, DW_PE)
                for i in range(DW_PE):
                    ct, taps = DW_SIDE + 1 + i, TAPS - DW_SHARED if i == 0 else TAPS
                    pe.wait_ge(hb_ready, ct // 2 + 1)
                    if i == 0:
                        pe.wait_ge(cv_bias, 2 * CV_CHUNKS - 2)
                    for j in range(taps):
                        if i == 0 and j == taps - 2:
                            pe.wait_ge(cv_gated, 2 * CV_CHUNKS)
                            turn(TR + (CV_CHUNKS - 1) % 2, gated, 0).then_inc(cv_trans, 1)
                        last = nc.tensor.matmul(ps[:, DW_BANKS[i], 0:SEQ], diag[:, i, j, :],
                                                hb[:, ct, j:j + SEQ], start=(j == 0), stop=(j == taps - 1))
                    last.then_inc(dw_pe, 1)
                pe.wait_ge(const_made, 1)
                order = [0, 1, DW_SIDE + 2, 2, 3, DW_SIDE, *range(DW_SIDE + 3, KT), DW_SIDE + 1]
                for n, ct in enumerate(order):
                    if ct < DW_DVE:
                        pe.wait_ge(dw_step, dw_last(ct))
                    elif ct == DW_SIDE:
                        pe.wait_ge(side_step, TAPS)
                    elif ct == DW_SIDE + 1:
                        pe.wait_ge(dw_step, DW_STEPS + DW_SHARED + 1)
                    else:
                        pe.wait_ge(dw_out, ct - DW_SIDE - 1)
                    last = nc.tensor.matmul(ps[:, 6, 0:SEQ], mean_w[:, :], cvo[:, ct, :],
                                            start=(n == 0), stop=(n == KT - 1))
                last.then_inc(mean_done, 1)
                keep_busy(4)
                for ct in range(KT):
                    if ct % 2 == 0:
                        pe.wait_ge(cv_squares, ct // 2 + 1)
                    for t in range(TOKS):
                        last = nc.tensor.matmul(ps[:, DW_BANKS[t], 0:P], cvs[:, ct, t * P:t * P + P], mean_w[:, :],
                                                start=(ct == 0), stop=(ct == KT - 1))
                last.then_inc(var_done, 1)
                keep_busy(3)
                pe.wait_ge(ln_spread, TOKS)
                for t in range(TOKS):
                    last = nc.tensor.matmul(ps[:, 7, t * P:t * P + P], mean_w[:, :], ln_diag[:, t, :],
                                            start=True, stop=True)
                last.then_inc(ln_rstd_done, 1)
                keep_busy(6)
                for k in range(4):
                    u = U_CONV + 2 * CV_CHUNKS + k

                    def inputs(j):
                        pe.wait_ge(z_hi, 2 * k + j + 1)
                        pe.wait_ge(z_lo, 2 * k + j + 1)

                    down_unit(u, u % SLOTS, xhi, xlo, 2 * k, k == 0, final=k == 3, inputs=inputs,
                              between={3: first_transposes(2)} if k == 3 else None)

            def gla():
                def unit(k, bank, phase=None, between=None):
                    u = U_GLA + k
                    wide_unit(u, u % SLOTS, k % 2, bank, phase, between)

                def gate_logits():
                    pe.wait_ge(aT_ready, 1)
                    for hd in range(HEADS):
                        last = nc.tensor.matmul(ps[:, 4 + hd // 2, (hd % 2) * SEQ:(hd % 2) * SEQ + SEQ],
                                                a2_sb[:, hd * HK:hd * HK + HK], aT[0:16, :], start=True, stop=True)
                    last.then_inc(a2_done, 1)

                def turn_q():
                    pe.wait_ge(qk_tok, 2)
                    for b in range(2):
                        turn(TR + b, q_tok, b * 256).then_inc(qk_trans, 1)

                def turn_k():
                    pe.wait_ge(k_scaled, TOKS)
                    for b in range(2):
                        pe.wait_ge(qkT_ready, b + 1)
                        turn(TR + b, k_tok, b * 256).then_inc(qk_trans, 1)

                def score(i):
                    def do():
                        hd, tile = i // 2, i % 2
                        bank = 4 + 2 * (i % 2)
                        if i >= 2:
                            pe.wait_ge(masked_ready, i - 1)
                            if tile == 0:
                                pe.wait_ge(cross_ready, hd)
                        if i == 0:
                            pe.wait_ge(qkT_ready, 4)
                            pe.wait_ge(zb_ready, HEADS)
                        s0 = hd * SEQ + tile * P
                        nc.tensor.matmul(ps[:, bank, 0:P], kT[:, hd, tile * P:tile * P + P],
                                         qT[:, hd, tile * P:tile * P + P], start=True, stop=True)
                        for lv in range(LEVELS - 2):
                            if i == 0:
                                pe.wait_ge(qk_ready, 2 * (lv + 1))
                            at = lv + 1
                            both = qk[:, lv, s0:s0 + P]
                            nc.tensor.matmul(ps[:, bank + at // 4, (at % 4) * P:(at % 4) * P + P],
                                             both, both, start=True, stop=True)
                        if i == 0:
                            pe.wait_ge(qk_ready, 2 * LEVELS)
                        last = nc.tensor.matmul(ps[0:64, bank + 1, 2 * P + 64:3 * P], qk[:, LEVELS - 2, s0:s0 + 64],
                                                qk[:, LEVELS - 2, s0 + 64:s0 + P], start=True, stop=True)
                        if tile == 0:
                            last = nc.tensor.matmul(ps[:, bank + 1, 3 * P:4 * P],
                                                    qk[:, LEVELS - 1, hd * SEQ:hd * SEQ + P],
                                                    qk[:, LEVELS - 1, hd * SEQ + P:hd * SEQ + SEQ],
                                                    start=True, stop=True)
                        last.then_inc(scores, 1)
                    return do

                def values(hd):
                    def do():
                        bank = hd % 2
                        pe.wait_ge(attn_ready, 2 * hd + 2)
                        pe.wait_ge(cross_ready, hd + 1)
                        if hd < 2:
                            pe.wait_ge(r_biased, 2)
                        else:
                            pe.wait_ge(y_lo, 2 * (hd - 1))
                        vc = slice(hd * HV, hd * HV + HV)
                        nc.tensor.matmul(ps[:, bank, 0:HV], attn[:, 3 * hd, :], v_sb[:, 0, vc], start=True, stop=True)
                        nc.tensor.matmul(ps[:, bank, HV:2 * HV], attn[:, 3 * hd + 2, :], v_sb[:, 0, vc],
                                         start=True, stop=False)
                        nc.tensor.matmul(ps[:, bank, HV:2 * HV], attn[:, 3 * hd + 1, :], v_sb[:, 1, vc],
                                         start=False, stop=True).then_inc(o_done, 1)
                    return do

                def turn_y(hd):
                    def do():
                        pe.wait_ge(y_ready, 2 * (hd + 1))
                        turn(hd % 2, y_tok, hd * HV).then_inc(y_trans, 1)
                    return do

                def out_unit(hd, **how):
                    u = U_GLA + 12 + hd
                    if hd == 0:
                        pe.wait_ge(masked_ready, 2 * HEADS - 1)
                        pe.wait_ge(cross_ready, HEADS)
                    pe.wait_ge(y_hi, 2 * (hd + 1))
                    pe.wait_ge(y_lo, 2 * (hd + 1))
                    down_unit(u, u % SLOTS, xhi, xlo, 2 * hd, hd == 0, **how)

                def r_read_out():
                    pe.wait_ge(r_biased, 4)
                    values(2)()

                unit(0, 0, 4)
                unit(1, 0, 4)
                pe.wait_ge(a1_split, 2)
                for kt in range(KT):
                    w = slice(kt * 16, kt * 16 + 16)
                    last = three(ps[0:16, 4, 0:SEQ], a1_hi[:, w], a1_lo[:, w], xhi[:, kt, :], xlo[:, kt, :],
                                 kt == 0, kt == KT - 1)
                last.then_inc(za_done, 1)
                pe.wait_ge(norm_diag, TOKS)
                for t in range(TOKS):
                    last = nc.tensor.matmul(ps[0:16, 5, t * P:t * P + P], mean_w[:, 0:16], rstd_diag[:, t, :],
                                            start=True, stop=True)
                last.then_inc(norm_spread, 1)
                unit(2, 2, between={2: gate_logits})
                unit(3, 2, between={0: turn_q})
                unit(4, 0, between={2: turn_k})
                unit(5, 0)
                pe.wait_ge(k_scaled, TOKS)
                unit(6, 2)
                unit(7, 2)
                pe.wait_ge(v_ready, 2)
                unit(8, 0, between={3: score(0)})
                unit(9, 0, between={0: score(1), 2: score(2)})
                pe.wait_ge(v_ready, 4)
                unit(10, 2, between={0: score(3), 2: score(4), 3: values(0)})
                unit(11, 2, between={0: score(5), 1: values(1), 2: score(6), 3: turn_y(0)})
                score(7)()
                out_unit(0, order=[(0, 1), (1, 1), (0, 0), (1, 0)],
                         between={1: turn_y(1), 2: r_read_out, 3: values(3)})
                out_unit(1, between={1: turn_y(2), 3: turn_y(3)})
                out_unit(2)
                out_unit(3, final=True, between={3: first_transposes(5)})

            pe.wait_ge(const_made, 1)
            keep_busy(6)
            pe.wait_ge(ident_loaded, 16)
            first_transposes(0)()
            keep_busy(4)
            ffn(0)
            conv()
            ffn(1)
            ffn(2)
            gla()
            ffn(3)

        @block.scalar
        def _(act):
            def convert(u):
                if u >= UNITS:
                    return
                slot = u % SLOTS
                if u >= SLOTS:
                    act.wait_ge(unit_used, u - SLOTS + 1)
                act.wait_ge(raw_landed[slot], 16 * (u // SLOTS))
                nc.scalar.copy(whi[:, slot, :], raw[:, slot, :]).then_inc(hi_made, 1)

            def convert_in_loop(u0, n, k):
                slot = (u0 + k) % SLOTS
                act.wait_ge(unit_used, u0 + 3 * n + k - SLOTS + 1)
                act.wait_ge(raw_landed[slot], 16 * ((u0 + k) // SLOTS) + 16 * n)
                nc.scalar.copy(whi[:, slot, :], raw[:, slot, :]).then_inc(hi_made, 1)

            def norm_in(phase):
                for kt in range(KT):
                    act.wait_ge(x_trans, KT * phase + kt + 1)
                    at = (kt // 2) % 2 * SEQ
                    nc.scalar.activation(xhi[:, kt, :], ps[:, TR + kt % 2, at:at + SEQ], ACT.Copy,
                                         scale=chan_sb[:, C_NORM + phase * KT + kt:C_NORM + phase * KT + kt + 1]
                                         ).then_inc(x_hi, 1)
                    if phase == 0:
                        for k in QUARTERS_AFTER.get(kt, []):
                            first_piece(k)
                    elif kt == 3:
                        convert(START[phase] + 2)
                    if kt == 5:
                        row_squares(phase, 0)
                    if kt == (6 if phase == 0 else 7):
                        row_squares(phase, 1)

            def first_piece(k):
                c = slice(k % 4 * 512, k % 4 * 512 + 512)
                act.wait_ge(piece_landed[k], 16)
                nc.scalar.copy(whi[:, k // 4, c], raw[:, k // 4, c]).then_inc(hi_piece, 1)
                if k % 4 == 3:
                    act.wait_ge(hi_piece, k + 1)
                    act.sem_inc(hi_made, 1)

            def row_squares(phase, t):
                if phase:
                    act.wait_ge(h_added, 4 * phase)
                if phase or t:
                    act.wait_ge(squares_done, TOKS * phase + t)
                nc.scalar.activation(squares[:, :], h[:, t, :], ACT.Square, scale=D ** -0.5,
                                     accum_out=mean_sq[:, t:t + 1]).then_inc(squares_done, 1)

            def ffn(f):
                phase, u0 = PHASE_OF_FFN[f], U_FFN[f]
                g0 = f * CHUNKS

                def silu(n):
                    done = u0 + 2 if isinstance(n, int) and n == 0 else u0 + 3 * n + 1
                    act.wait_ge(unit_used, done)
                    bank = DN if isinstance(n, int) and n == 0 else GU
                    for t in range(TOKS):
                        nc.scalar.activation(silu_g[:, t, :], ps[:, bank + t, 0:256], ACT.Silu,
                                             scale=rstd[:, t:t + 1]).then_inc(silu_done, 1)

                def high_of_gated(n, dst=ghi[:, :, :]):
                    act.wait_ge(g_trans, g0 + n + 1)
                    nc.scalar.copy(dst.rearrange("p a b -> p (a b)"), ps[:, TR, :]).then_inc(g_hi, 1)

                norm_in(phase)
                act.wait_ge(rstd_ready, phase + 1)
                if f == 0:
                    silu(0)
                    convert(3)
                else:
                    convert(u0 + 3)
                    silu(0)
                convert(u0 + 4)
                with act.Fori(1, CHUNKS - 1) as n:
                    high_of_gated(n - 1)
                    convert_in_loop(u0, n, 2)
                    silu(n)
                    convert_in_loop(u0, n, 3)
                    convert_in_loop(u0, n, 4)
                n = CHUNKS - 1
                high_of_gated(n - 1)
                convert(u0 + 3 * n + 2)
                silu(n)
                convert(u0 + 3 * n + 3)
                high_of_gated(n, xhi[:, KT - 2:KT, :])
                convert(u0 + 3 * n + 4)

            def conv():
                norm_in(1)

                def side_first():
                    at = C_DW + DW_SIDE * TAPS
                    nc.scalar.activation(cvo[:, DW_SIDE, :], hb[:, DW_SIDE, 0:SEQ], ACT.Identity,
                                         scale=chan_sb[:, at:at + 1],
                                         bias=chan_sb[:, C_BDW + DW_SIDE:C_BDW + DW_SIDE + 1]).then_inc(side_step, 1)

                def side_products(turn, waits):
                    for k in range(SIDE_TAPS):
                        if waits:
                            act.wait_ge(side_step, turn * SIDE_TAPS + (k + 2 - SIDE_TAPS))
                        tap = turn * SIDE_TAPS + (C_DW + DW_SIDE * TAPS + 1 + k)
                        nc.scalar.activation(cvs[:, k, :], hb[:, DW_SIDE, bass.ds(turn * SIDE_TAPS + (1 + k), SEQ)],
                                             ACT.Copy, scale=chan_sb[:, bass.ds(tap, 1)]).then_inc(side_product, 1)

                for c in range(CV_CHUNKS):
                    u = U_CONV + 2 * c
                    convert(u + 3)
                    if c >= 1:
                        channels_in(c - 1)
                    if c == CV_CHUNKS - 1:
                        act.wait_ge(hb_ready, DW_SIDE // 2 + 1)
                        side_first()
                        side_products(0, False)
                    for t in range(TOKS):
                        act.wait_ge(cv_bias, 2 * c + t + 1)
                        nc.scalar.activation(sg[:, t, :], ag[:, t, 256:512], ACT.Sigmoid).then_inc(cv_sig, 1)
                    if c < CV_CHUNKS - 1:
                        convert(u + 4)
                channels_in(CV_CHUNKS - 1)
                with act.Fori(1, (TAPS - 1) // SIDE_TAPS) as turn:
                    side_products(turn, True)
                convert(U_CONV + 10)
                for i in range(1, DW_PE):
                    ct = DW_SIDE + 1 + i
                    act.wait_ge(dw_pe, i + 1)
                    nc.scalar.activation(cvo[:, ct, :], ps[:, DW_BANKS[i], 0:SEQ], ACT.Identity,
                                         bias=chan_sb[:, C_BDW + ct:C_BDW + ct + 1]).then_inc(dw_out, 1)
                for j in range(4):
                    act.wait_ge(centred, j + 1)
                    nc.scalar.activation(cvs[:, 2 * j:2 * j + 2, :], cvo[:, 2 * j:2 * j + 2, :],
                                         ACT.Square).then_inc(cv_squares, 1)
                for ct in range(KT):
                    act.wait_ge(normed, ct + 1)
                    nc.scalar.activation(cvs[:, ct, :], cvo[:, ct, :], ACT.Silu,
                                         bias=chan_sb[:, C_LNB + ct:C_LNB + ct + 1],
                                         scale=chan_sb[:, C_LNG + ct:C_LNG + ct + 1]).then_inc(cv_act, 1)
                    act.wait_ge(cv_act, ct + 1)
                    nc.scalar.copy(xhi[:, ct, :], cvs[:, ct, :]).then_inc(z_hi, 1)
                convert(U_CONV + 11)
                convert(U_CONV + 12)
                convert(U_CONV + 13)

            def channels_in(c):
                act.wait_ge(cv_trans, c + 1)
                if c == 0:
                    act.wait_ge(hb_zero, 1)
                nc.scalar.copy(hb[:, 2 * c:2 * c + 2, PAD:PAD + SEQ],
                               ps[:, TR + c % 2, :].rearrange("p (a b) -> p a b", a=2)).then_inc(hb_ready, 1)

            def gla():
                U = U_GLA
                norm_in(4)
                act.wait_ge(rstd_ready, 5)
                convert(U + 3)

                def scaled(k, bank, dst, c0, signal):
                    act.wait_ge(unit_used, U + k + 1)
                    for t in range(TOKS):
                        nc.scalar.activation(dst[:, t, c0:c0 + 512], ps[:, bank + t, :], ACT.Copy,
                                             scale=rstd[:, t:t + 1]).then_inc(signal, 1)

                def decay(lv):
                    act.wait_ge(dif_ready, 2 * (lv + 1))
                    nc.scalar.activation(dif[lv % 3], dif[lv % 3], ACT.Exp, scale=1.0 / TAU).then_inc(decay_ready, 1)

                def r_gate(c):
                    act.wait_ge(r_biased, 2 * (c + 1))
                    nc.scalar.activation(rg[:, :, c * 512:c * 512 + 512], rg[:, :, c * 512:c * 512 + 512],
                                         ACT.Silu).then_inc(r_silu, 1)

                def head_squares(hd):
                    act.wait_ge(o_done, hd + 1)
                    for t in range(TOKS):
                        if hd or t:
                            act.wait_ge(o_squares, 2 * hd + t)
                        nc.scalar.activation(o_sq, ps[:, hd % 2, t * HV:t * HV + HV], ACT.Square, scale=HV ** -0.5,
                                             accum_out=o_ms[:, 2 * hd + t:2 * hd + t + 1]).then_inc(o_squares, 1)

                def high_of_y(hd):
                    if hd == 0:
                        act.wait_ge(unit_used, U + 12)
                    act.wait_ge(y_trans, hd + 1)
                    for k in range(2):
                        nc.scalar.activation(xhi[:, 2 * hd + k, :], ps[:, hd % 2, k * SEQ:k * SEQ + SEQ], ACT.Copy,
                                             scale=chan_sb[:, C_NG + k:C_NG + k + 1]).then_inc(y_hi, 1)

                scaled(1, 0, q_tok, 0, qk_tok)
                act.wait_ge(za_done, 1)
                nc.scalar.copy(za[0:16, :], ps[0:16, 4, 0:SEQ]).then_inc(za_copied, 1)
                convert(U + 4)
                act.wait_ge(zb_ready, HEADS)
                nc.scalar.activation(dif0, zb, ACT.Abs).then_inc(soft, 1)
                convert(U + 5)
                act.wait_ge(soft, 1)
                nc.scalar.activation(dif1, dif0, ACT.Exp, scale=-1.0).then_inc(soft, 1)
                act.wait_ge(soft, 2)
                nc.scalar.activation(dif0, dif1, ACT.Ln, bias=1.0).then_inc(soft, 1)
                for b in range(2):
                    act.wait_ge(qk_trans, b + 1)
                    nc.scalar.mul(qT[:, 2 * b:2 * b + 2, :], ps[:, TR + b, :].rearrange("p (a b) -> p a b", a=2),
                                  HK ** -0.5).then_inc(qkT_ready, 1)
                convert(U + 6)
                for b in range(2):
                    act.wait_ge(qk_trans, 2 + b + 1)
                    nc.scalar.copy(kT[:, 2 * b:2 * b + 2, :],
                                   ps[:, TR + b, :].rearrange("p (a b) -> p a b", a=2)).then_inc(qkT_ready, 1)
                decay(0)
                decay(1)
                decay(2)
                convert(U + 7)
                decay(3)
                decay(4)
                convert(U + 8)
                scaled(5, 0, v_sb, 0, v_ready)
                decay(5)
                decay(6)
                convert(U + 9)
                decay(7)
                convert(U + 10)
                scaled(7, 2, v_sb, 512, v_ready)
                convert(U + 11)
                convert(U + 12)
                r_gate(0)
                head_squares(0)
                convert(U + 13)
                head_squares(1)
                high_of_y(0)
                convert(U + 14)
                r_gate(1)
                high_of_y(1)
                head_squares(2)
                head_squares(3)
                convert(U + 15)
                high_of_y(2)
                high_of_y(3)
                convert(U + 16)
                convert(U + 17)

            START = [U_FFN[0], U_CONV, U_FFN[1], U_FFN[2], U_GLA, U_FFN[3]]
            act.dma_start(ident[:, :], ident_d).then_inc(ident_loaded, 16)
            act.dma_start(chan_sb[:, :], chan).then_inc(chan_loaded, 16)
            act.wait_ge(const_made, 2)
            nc.scalar.copy(ms[:, :], neg_half[:, :])
            act.wait_ge(chan_loaded, 16)
            ffn(0)
            conv()
            ffn(1)
            act.wait_ge(z_lo, KT)
            act.dma_start(mask_sb.rearrange("p a b -> p (a b)"), masks).then_inc(gla_loaded, 16)
            act.dma_start(a1_raw, a1).then_inc(gla_loaded, 16)
            act.dma_start(a2_sb, a2).then_inc(gla_loaded, 16)
            ffn(2)
            gla()
            ffn(3)
            for n, (t, half) in enumerate(((0, 0), (0, 1), (1, 0), (1, 1))):
                act.wait_ge(h_added, 4 * 5 + n + 1)
                act.wait_ge(squares_done, TOKS * 6 + n)
                c = slice(half * 512, half * 512 + 512)
                nc.scalar.activation(squares[:, c], h[:, t, c], ACT.Square, scale=D ** -0.5,
                                     accum_out=half_sq[:, n:n + 1]).then_inc(squares_done, 1)

        @block.vector
        def _(dve):
            def low(slot):
                nc.vector.tensor_tensor(wlo[:, slot, :], raw[:, slot, :], whi[:, slot, :].bitcast(F32),
                                        ALU.subtract).then_inc(lo_made, 1)

            def convert(u):
                if u >= UNITS:
                    return
                dve.wait_ge(hi_made, u + 1)
                if u - 1 in POOL_UNITS:
                    dve.wait_ge(lo_made, u)
                low(u % SLOTS)

            def convert_in_loop(u0, n, k):
                dve.wait_ge(hi_made, u0 + 3 * n + k + 1)
                low((u0 + k) % SLOTS)

            def norm_low(phase, kts):
                for kt in kts:
                    dve.wait_ge(x_hi, KT * phase + kt + 1)
                    at = (kt // 2) % 2 * SEQ
                    nc.vector.scalar_tensor_tensor(
                        out=xlo[:, kt, :], in0=ps[:, TR + kt % 2, at:at + SEQ],
                        scalar=chan_sb[:, C_NORM + phase * KT + kt:C_NORM + phase * KT + kt + 1],
                        in1=xhi[:, kt, :].bitcast(F32), op0=ALU.mult, op1=ALU.subtract).then_inc(x_lo, 1)

            def residual(phase, factor, last_unit):
                for n, (half, t) in enumerate(((0, 0), (1, 0), (0, 1), (1, 1)) if phase == 5
                                              else ((0, 0), (0, 1), (1, 0), (1, 1))):
                    if n < 3:
                        dve.wait_ge(down_part, 3 * phase + n + 1)
                    else:
                        if phase < 5:
                            norm_low(phase + 1, (0, 1))
                        dve.wait_ge(unit_used, last_unit + 1)
                    c = slice(half * 512, half * 512 + 512)
                    nc.vector.scalar_tensor_tensor(out=h[:, t, c], in0=ps[:, DN + 2 * t + half, :], scalar=factor,
                                                   in1=h[:, t, c], op0=ALU.mult, op1=ALU.add).then_inc(h_added, 1)
                if phase == 5:
                    final_norm(0)
                    final_norm(1)

            def final_norm(t):
                if t == 0:
                    dve.wait_ge(gain_loaded, 16)
                dve.wait_ge(rstd_ready, 6 + t + 1)
                for half in range(2):
                    c = slice(half * 512, half * 512 + 512)
                    nc.vector.scalar_tensor_tensor(out=h[:, t, c], in0=h[:, t, c], scalar=rstd[:, t:t + 1],
                                                   in1=pair[:, c], op0=ALU.mult, op1=ALU.mult).then_inc(out_ready, 1)

            def norm_in(phase):
                if phase == 0:
                    for kt in range(KT):
                        norm_low(0, (kt,))
                        for k in QUARTERS_AFTER.get(kt, []):
                            first_piece(k)
                else:
                    norm_low(phase, range(2, 6))
                    convert(START[phase] + 2)
                    norm_low(phase, (6, 7))

            def first_piece(k):
                s, c = k // 4, slice(k % 4 * 512, k % 4 * 512 + 512)
                dve.wait_ge(hi_piece, k + 1)
                nc.vector.tensor_tensor(wlo[:, s, c], raw[:, s, c], whi[:, s, c].bitcast(F32),
                                        ALU.subtract).then_inc(lo_piece, 1)
                if k % 4 == 3:
                    dve.wait_ge(lo_piece, k + 1)
                    dve.sem_inc(lo_made, 1)

            def ffn(f):
                phase, u0 = PHASE_OF_FFN[f], U_FFN[f]
                g0 = f * CHUNKS

                def gate(n):
                    bank = DN if isinstance(n, int) and n == 0 else GU
                    for t in range(TOKS):
                        dve.wait_ge(silu_done, 2 * (g0 + n) + t + 1)
                        nc.vector.scalar_tensor_tensor(out=gated[:, t, :], in0=ps[:, bank + t, 256:512],
                                                       scalar=rstd[:, t:t + 1], in1=silu_g[:, t, :],
                                                       op0=ALU.mult, op1=ALU.mult).then_inc(gated_done, 1)

                def low_of_gated(n, dst=glo[:, :, :], high=ghi[:, :, :]):
                    dve.wait_ge(g_hi, g0 + n + 1)
                    nc.vector.tensor_tensor(dst.rearrange("p a b -> p (a b)"), ps[:, TR, :],
                                            high.rearrange("p a b -> p (a b)").bitcast(F32),
                                            ALU.subtract).then_inc(g_lo, 1)

                norm_in(phase)
                if f == 0:
                    gate(0)
                    convert(3)
                else:
                    convert(u0 + 3)
                    gate(0)
                convert(u0 + 4)
                with dve.Fori(1, CHUNKS - 1) as n:
                    low_of_gated(n - 1)
                    convert_in_loop(u0, n, 2)
                    gate(n)
                    convert_in_loop(u0, n, 3)
                    convert_in_loop(u0, n, 4)
                n = CHUNKS - 1
                low_of_gated(n - 1)
                convert(u0 + 3 * n + 2)
                gate(n)
                convert(u0 + 3 * n + 3)
                low_of_gated(n, xlo[:, KT - 2:KT, :], xhi[:, KT - 2:KT, :])
                residual(phase, 0.5, u0 + FFN_UNITS - 1)

            def conv():
                norm_in(1)
                dve.wait_ge(rstd_ready, 2)
                dve.wait_ge(bias_loaded, 32)

                def low_of_z(ct):
                    dve.wait_ge(z_hi, ct + 1)
                    nc.vector.tensor_tensor(xlo[:, ct, :], cvs[:, ct, :], xhi[:, ct, :].bitcast(F32),
                                            ALU.subtract).then_inc(z_lo, 1)

                def first_taps(ct0, n):
                    for ct in range(ct0, ct0 + n):
                        dve.wait_ge(hb_ready, ct // 2 + 1)
                        nc.vector.tensor_scalar(cvo[:, ct, :], hb[:, ct, 0:SEQ],
                                                chan_sb[:, C_DW + ct * TAPS:C_DW + ct * TAPS + 1],
                                                chan_sb[:, C_BDW + ct:C_BDW + ct + 1],
                                                ALU.mult, ALU.add).then_inc(dw_step, 1)

                def taps(run):
                    ct0, n, a, b, per_turn = DW_RUNS[run]
                    base = dw_before(run)
                    assert (b - a) % per_turn == 0
                    with dve.Fori(0, (b - a) // per_turn) as turn:
                        for k in range(per_turn):
                            for i in range(n):
                                ct = ct0 + i
                                dve.wait_ge(dw_step, turn * (n * per_turn) + (base + n * (k - 1) + i + 1))
                                nc.vector.scalar_tensor_tensor(
                                    out=cvo[:, ct, :], in0=hb[:, ct, bass.ds(turn * per_turn + (a + k), SEQ)],
                                    scalar=chan_sb[:, bass.ds(turn * per_turn + (C_DW + ct * TAPS + a + k), 1)],
                                    in1=cvo[:, ct, :], op0=ALU.mult, op1=ALU.add).then_inc(dw_step, 1)

                for c in range(CV_CHUNKS):
                    u = U_CONV + 2 * c
                    if c == 1:
                        first_taps(0, 2)
                    if c:
                        taps(c - 1)
                    dve.wait_ge(unit_used, u + 2)
                    for t in range(TOKS):
                        if c:
                            dve.wait_ge(cv_gated, 2 * (c - 1) + t + 1)
                        nc.vector.scalar_tensor_tensor(out=ag[:, t, :], in0=ps[:, 2 * (c % 2) + t, :],
                                                       scalar=rstd[:, t:t + 1], in1=cvb[:, c * 512:c * 512 + 512],
                                                       op0=ALU.mult, op1=ALU.add).then_inc(cv_bias, 1)
                    if c:
                        dve.wait_ge(cv_trans, c)
                    for t in range(TOKS):
                        dve.wait_ge(cv_sig, 2 * c + t + 1)
                        nc.vector.tensor_tensor(gated[:, t, :], ag[:, t, 0:256], sg[:, t, :],
                                                ALU.mult).then_inc(cv_gated, 1)
                first_taps(2, DW_DVE - 2)
                taps(3)
                ct = DW_SIDE + 1
                for n in range(DW_SHARED):
                    j = TAPS - DW_SHARED + n
                    tap = chan_sb[:, C_DW + ct * TAPS + j:C_DW + ct * TAPS + j + 1]
                    if n == 0:
                        nc.vector.tensor_scalar(cvo[:, ct, :], hb[:, ct, j:j + SEQ], tap,
                                                chan_sb[:, C_BDW + ct:C_BDW + ct + 1],
                                                ALU.mult, ALU.add).then_inc(dw_step, 1)
                    else:
                        dve.wait_ge(dw_step, DW_STEPS + n)
                        nc.vector.scalar_tensor_tensor(out=cvo[:, ct, :], in0=hb[:, ct, j:j + SEQ], scalar=tap,
                                                       in1=cvo[:, ct, :], op0=ALU.mult, op1=ALU.add).then_inc(dw_step, 1)
                dve.wait_ge(dw_step, DW_STEPS + DW_SHARED)
                dve.wait_ge(dw_pe, 1)
                nc.vector.tensor_tensor(cvo[:, ct, :], cvo[:, ct, :], ps[:, DW_BANKS[0], 0:SEQ],
                                        ALU.add).then_inc(dw_step, 1)
                dve.wait_ge(mean_done, 1)
                for j in range(4):
                    nc.vector.tensor_tensor(cvo[:, 2 * j:2 * j + 2, :], cvo[:, 2 * j:2 * j + 2, :],
                                            ps[:, 6, 0:SEQ].unsqueeze(1).to_broadcast([P, 2, SEQ]),
                                            ALU.subtract).then_inc(centred, 1)
                dve.wait_ge(var_done, 1)
                for t in range(TOKS):
                    nc.vector.tensor_scalar(ln_var[:, t:t + 1], ps[:, DW_BANKS[t], 0:1], EPS, None,
                                            ALU.add).then_inc(ln_var_ready, 1)
                dve.wait_ge(ln_pow_done, 1)
                for t in range(TOKS):
                    nc.vector.tensor_scalar(ln_diag[:, t, :], ident[:, :], ln_rstd[:, t:t + 1], float(D),
                                            ALU.mult, ALU.mult).then_inc(ln_spread, 1)
                dve.wait_ge(ln_rstd_done, 1)
                for ct in range(KT):
                    nc.vector.tensor_tensor(cvo[:, ct, :], cvo[:, ct, :], ps[:, 7, 0:SEQ],
                                            ALU.mult).then_inc(normed, 1)
                    if ct >= 3:
                        low_of_z(ct - 3)
                for ct in range(KT - 3, KT):
                    low_of_z(ct)
                convert(U_CONV + 11)
                convert(U_CONV + 12)
                dve.wait_ge(bias_added, 1)
                residual(1, 1.0, U_CONV + CV_UNITS - 1)

            def gla():
                U = U_GLA

                def difference(lv):
                    m = 2 ** lv
                    b = b64 if m <= 32 else b256
                    bv = b.rearrange("p a b -> p (a b)").rearrange("p (g two m) -> p g two m", two=2, m=m)
                    dv = dif[lv % 3].rearrange("p a b -> p (a b)").rearrange("p (g two m) -> p g two m", two=2, m=m)
                    groups = HEADS * SEQ // (2 * m)
                    mid = bv[:, :, 0, m - 1:m].to_broadcast([P, groups, m])
                    if lv >= 3:
                        dve.wait_ge(qk_ready, 2 * (lv - 2))
                    nc.vector.tensor_tensor(dv[:, :, 0, :], mid, bv[:, :, 0, :], ALU.subtract).then_inc(dif_ready, 1)
                    nc.vector.tensor_tensor(dv[:, :, 1, :], bv[:, :, 1, :], mid, ALU.subtract).then_inc(dif_ready, 1)

                def running(b, keep):
                    for hd in range(HEADS):
                        nc.vector.tensor_tensor_scan(b[:, hd, :], keep, zb[:, hd, :], 0.0,
                                                     ALU.mult, ALU.add).then_inc(scanned, 1)

                def r_bias(c):
                    dve.wait_ge(unit_used, U + 9 + 2 * c + 1)
                    for t in range(TOKS):
                        nc.vector.scalar_tensor_tensor(out=rg[:, t, c * 512:c * 512 + 512], in0=ps[:, 2 * c + t, :],
                                                       scalar=rstd[:, t:t + 1], in1=rows_sb[:, c * 512:c * 512 + 512],
                                                       op0=ALU.mult, op1=ALU.add).then_inc(r_biased, 1)

                def attention(i):
                    hd, tile = i // 2, i % 2
                    bank = 4 + 2 * (i % 2)
                    dve.wait_ge(scores, i + 1)
                    if i >= 2:
                        dve.wait_ge(attn_ready, i - 1)
                    mk = masked[i % 2][:, 0:MASKS, :]
                    nc.vector.tensor_tensor(
                        mk, ps[:, bank:bank + 2, :].rearrange("p a (l t) -> p (a l) t", t=P)[:, 0:MASKS, :],
                        mask_sb[:, :, :], ALU.mult).then_inc(masked_ready, 1)
                    if i == 0:
                        dve.wait_ge(qk_ready, 2 * LEVELS)
                    if tile == 0:
                        nc.vector.tensor_copy(attn[:, 3 * hd + 2, :],
                                              ps[:, bank + 1, 3 * P:4 * P]).then_inc(cross_ready, 1)
                    dve.wait_ge(masked_ready, i + 1)
                    nc.vector.tensor_reduce(attn[:, 3 * hd + tile, :], mk.rearrange("p l t -> p t l"),
                                            AX_X, ALU.add).then_inc(attn_ready, 1)

                def gated_output(hd):
                    dve.wait_ge(o_rstd_done, hd + 1)
                    dve.wait_ge(r_silu, hd // 2 + 1)
                    for t in range(TOKS):
                        c = slice(hd * HV, hd * HV + HV)
                        nc.vector.scalar_tensor_tensor(
                            out=y_tok[:, t, c], in0=ps[:, hd % 2, t * HV:t * HV + HV],
                            scalar=o_rstd[:, 2 * hd + t:2 * hd + t + 1], in1=rg[:, t, c],
                            op0=ALU.mult, op1=ALU.mult).then_inc(y_ready, 1)

                def low_of_y(hd):
                    dve.wait_ge(y_hi, 2 * hd + 2)
                    for k in range(2):
                        nc.vector.scalar_tensor_tensor(
                            out=xlo[:, 2 * hd + k, :], in0=ps[:, hd % 2, k * SEQ:k * SEQ + SEQ],
                            scalar=chan_sb[:, C_NG + k:C_NG + k + 1], in1=xhi[:, 2 * hd + k, :].bitcast(F32),
                            op0=ALU.mult, op1=ALU.subtract).then_inc(y_lo, 1)

                norm_in(4)
                convert(U + 3)
                dve.wait_ge(rstd_ready, 5)
                for t in range(TOKS):
                    nc.vector.tensor_scalar(rstd_diag[:, t, :], ident[:, :], rstd[:, t:t + 1], float(D),
                                            ALU.mult, ALU.mult).then_inc(norm_diag, 1)
                dve.wait_ge(za_copied, 1)
                dve.wait_ge(norm_spread, 1)
                nc.vector.tensor_tensor(aT[0:16, :], za[0:16, :], ps[0:16, 5, 0:SEQ], ALU.mult).then_inc(aT_ready, 1)
                convert(U + 4)
                dve.wait_ge(a2_done, 1)
                for hd in range(HEADS):
                    nc.vector.tensor_scalar(zb[:, hd, :], ps[:, 4 + hd // 2, (hd % 2) * SEQ:(hd % 2) * SEQ + SEQ],
                                            chan_sb[:, C_BA + hd:C_BA + hd + 1], None, ALU.add).then_inc(zb_ready, 1)
                convert(U + 5)
                dve.wait_ge(unit_used, U + 4)
                for t in range(TOKS):
                    nc.vector.tensor_scalar(k_tok[:, t, :], ps[:, 2 + t, :], rstd[:, t:t + 1], None,
                                            ALU.mult).then_inc(k_scaled, 1)
                dve.wait_ge(soft, 3)
                nc.vector.scalar_tensor_tensor(out=zb, in0=zb, scalar=0.0, in1=dif0,
                                               op0=ALU.min, op1=ALU.subtract).then_inc(la_ready, 1)
                dve.wait_ge(keep_ready, 3)
                dve.wait_ge(la_ready, 1)
                running(b64, keep64)
                dve.wait_ge(scanned, HEADS)
                difference(0)
                difference(1)
                running(b256, keep_all)
                dve.wait_ge(scanned, 2 * HEADS)
                difference(2)
                convert(U + 6)
                difference(3)
                difference(4)
                convert(U + 7)
                difference(5)
                convert(U + 8)
                difference(6)
                difference(7)
                convert(U + 9)
                convert(U + 10)
                dve.wait_ge(gla_loaded, 48)
                attention(0)
                attention(1)
                attention(2)
                r_bias(0)
                attention(3)
                attention(4)
                attention(5)
                gated_output(0)
                attention(6)
                gated_output(1)
                low_of_y(0)
                r_bias(1)
                attention(7)
                low_of_y(1)
                gated_output(2)
                gated_output(3)
                low_of_y(2)
                low_of_y(3)
                convert(U + 15)
                convert(U + 16)
                residual(4, 1.0, U + GLA_UNITS - 1)

            START = [U_FFN[0], U_CONV, U_FFN[1], U_FFN[2], U_GLA, U_FFN[3]]
            dve.wait_ge(chan_loaded, 16)
            ffn(0)
            conv()
            ffn(1)
            ffn(2)
            gla()
            ffn(3)

        @block.gpsimd
        def _(pool):
            nc.gpsimd.memset(mean_w[:, :], 1.0 / D).then_inc(const_made, 1)
            nc.gpsimd.memset(hb[:, :, 0:PAD], 0.0).then_inc(hb_zero, 1)

            def row_rstd(phase):
                pool.wait_ge(squares_done, TOKS * (phase + 1))
                nc.gpsimd.tensor_scalar(ms[:, :], mean_sq[:, :], EPS, None, ALU.add).then_inc(ms_done, 1)
                pool.wait_ge(ms_done, phase + 1)
                nc.gpsimd.tensor_tensor(rstd[:, :], ms[:, :], neg_half[:, :], ALU.pow).then_inc(rstd_ready, 1)

            def low(u):
                slot = u % SLOTS
                pool.wait_ge(hi_made, u + 1)
                pool.wait_ge(lo_made, u)
                nc.gpsimd.tensor_tensor(wlo[:, slot, :], raw[:, slot, :], whi[:, slot, :].bitcast(F32),
                                        ALU.subtract).then_inc(lo_made, 1)

            nc.gpsimd.memset(neg_half[:, :], -0.5).then_inc(const_made, 1)
            pool.wait_ge(const_made, 2)
            row_rstd(0)
            pool.wait_ge(ident_loaded, 16)
            pool.wait_ge(chan_loaded, 16)
            for i in range(DW_PE):
                ct = DW_SIDE + 1 + i
                nc.gpsimd.tensor_tensor(diag[:, i, :, :], ident[:, :].unsqueeze(1).to_broadcast([P, TAPS, P]),
                                        chan_sb[:, C_DW + ct * TAPS:C_DW + (ct + 1) * TAPS].unsqueeze(2)
                                        .to_broadcast([P, TAPS, P]), ALU.mult).then_inc(diag_made, 1)
            low(U_CONV + 1)
            row_rstd(1)
            pool.wait_ge(bias_loaded, 32)
            for u in range(U_CONV + 3, U_CONV + 10):
                low(u)
            with pool.Fori(0, (TAPS - 1) // SIDE_TAPS) as turn:
                for k in range(SIDE_TAPS):
                    pool.wait_ge(side_product, turn * SIDE_TAPS + (k + 1))
                    pool.wait_ge(side_step, turn * SIDE_TAPS + (k + 1))
                    nc.gpsimd.tensor_tensor(cvo[:, DW_SIDE, :], cvo[:, DW_SIDE, :], cvs[:, k, :],
                                            ALU.add).then_inc(side_step, 1)
            low(U_CONV + 10)
            pool.wait_ge(x_trans, 2 * KT)
            nc.gpsimd.tensor_tensor(h[:, :, :], h[:, :, :], cvb[:, 2 * D:3 * D].unsqueeze(1).to_broadcast([P, TOKS, D]),
                                    ALU.add).then_inc(bias_added, 1)
            pool.wait_ge(ln_var_ready, TOKS)
            nc.gpsimd.tensor_tensor(ln_rstd, ln_var, neg_half[:, :], ALU.pow).then_inc(ln_pow_done, 1)
            low(U_FFN[1] + 1)
            row_rstd(2)
            low(U_FFN[2] + 1)
            row_rstd(3)
            pool.wait_ge(gla_loaded, 48)
            nc.gpsimd.tensor_copy(a1_hi[:, :], a1_raw).then_inc(a1_split, 1)
            pool.wait_ge(a1_split, 1)
            nc.gpsimd.tensor_tensor(a1_lo[:, :], a1_raw, a1_hi[:, :].bitcast(F32),
                                    ALU.subtract).then_inc(a1_split, 1)
            nc.gpsimd.memset(keep64, 1.0).then_inc(keep_ready, 1)
            nc.gpsimd.memset(keep_all, 1.0).then_inc(keep_ready, 1)
            pool.wait_ge(keep_ready, 1)
            nc.gpsimd.memset(keep64.rearrange("p (c t) -> p c t", t=64)[:, :, 0:1], 0.0).then_inc(keep_ready, 1)
            low(U_GLA + 1)
            row_rstd(4)
            for lv in range(LEVELS):
                m = 2 ** lv
                pool.wait_ge(decay_ready, lv + 1)
                split = "p (g two m) -> p g two m"
                dv = dif[lv % 3].rearrange("p a b -> p (a b)").rearrange(split, two=2, m=m)
                ov = qk[:, lv, :].rearrange(split, two=2, m=m)
                for part, src in ((1, qT), (0, kT)):
                    if lv == 0:
                        pool.wait_ge(qkT_ready, 2 if part else 4)
                    sv = src.rearrange("p a b -> p (a b)").rearrange(split, two=2, m=m)
                    nc.gpsimd.tensor_tensor(ov[:, :, part, :], dv[:, :, part, :], sv[:, :, part, :],
                                            ALU.mult).then_inc(qk_ready, 1)

            def head_rstd(hd):
                pool.wait_ge(o_squares, 2 * (hd + 1))
                c = slice(2 * hd, 2 * hd + 2)
                nc.gpsimd.tensor_scalar(o_me[:, c], o_ms[:, c], EPS, None, ALU.add).then_inc(o_eps_added, 1)
                pool.wait_ge(o_eps_added, hd + 1)
                nc.gpsimd.tensor_tensor(o_rstd[:, c], o_me[:, c], neg_half[:, :], ALU.pow).then_inc(o_rstd_done, 1)

            low(U_GLA + 11)
            low(U_GLA + 12)
            head_rstd(0)
            low(U_GLA + 13)
            head_rstd(1)
            low(U_GLA + 14)
            head_rstd(2)
            head_rstd(3)
            low(U_FFN[3] + 1)
            row_rstd(5)
            for t in range(TOKS):
                pool.wait_ge(squares_done, TOKS * 6 + 2 * t + 2)
                nc.gpsimd.tensor_scalar(ms[:, t:t + 1], half_sq[:, 2 * t:2 * t + 1], half_sq[:, 2 * t + 1:2 * t + 2],
                                        EPS, ALU.add, ALU.add).then_inc(ms_done, 1)
                pool.wait_ge(ms_done, 6 + t + 1)
                nc.gpsimd.tensor_tensor(rstd[:, t:t + 1], ms[:, t:t + 1], neg_half[:, 0:1],
                                        ALU.pow).then_inc(rstd_ready, 1)


INS = ["stream", "x", "chan", "rows", "a1", "a2", "masks", "ident"]


def level_masks():
    s, t = np.arange(P)[:, None], np.arange(P)[None, :]
    out = [s == t]
    for lv in range(LEVELS - 1):
        m = 2 ** lv
        out.append((s // (2 * m) == t // (2 * m)) & (s // m % 2 == 0) & (t // m % 2 == 1))
    out[-2:] = [out[-2] | out[-1]]
    return np.stack(out, axis=1).astype(np.float32).reshape(P, MASKS * P)


def kernel(**inputs):
    import concourse.bacc as _bacc
    from concourse.bass_utils import run_bass_kernel_spmd as _run

    a = {k: np.asarray(v) for k, v in inputs.items()}

    def wide(left, right, chunk):
        n = left.shape[1] // chunk
        both = [w.reshape(2, 4, P, n, chunk) for w in (left, right)]
        both = np.concatenate(both, axis=4)
        return both.transpose(3, 0, 2, 1, 4).reshape(2 * n, P, UNIT)

    def single(w):
        return w.reshape(2, 4, P, w.shape[1] // 512, 512).transpose(3, 0, 2, 1, 4).reshape(-1, P, UNIT)

    def down(w):
        return w.reshape(-1, 2, P, D).transpose(0, 2, 1, 3).reshape(-1, P, UNIT)

    def ffn(name, i):
        gu = wide(a[name + "_gate"][i], a[name + "_up"][i], 256).reshape(CHUNKS, 2, P, UNIT)
        dn = down(a[name + "_down"][i])
        parts = [gu[0]]
        for n in range(1, CHUNKS):
            parts += [gu[n], dn[n - 1:n]]
        return np.concatenate(parts + [dn[CHUNKS - 1:]])

    pw1 = a["cv_w_pw1"][0]
    stream = np.concatenate([
        ffn("w1", 0), wide(pw1[:, :D], pw1[:, D:], 256), down(a["cv_w_pw2"][0]), ffn("w2", 0), ffn("w1", 1),
        single(a["gla_w_q"][0]), single(a["gla_w_k"][0]), single(a["gla_w_v"][0]), single(a["gla_w_r"][0]),
        down(a["gla_w_o"][0]), ffn("w2", 1)])

    def col(v):
        return v.reshape(-1, P).T

    norms = [a["g_ffn1"][0], a["g_mix"][0], a["g_ffn2"][0], a["g_ffn1"][1], a["g_mix"][1], a["g_ffn2"][1]]
    dw = a["cv_w_dw"][0].reshape(TAPS, KT, P).transpose(2, 1, 0).reshape(P, KT * TAPS)
    chan = np.concatenate([col(v) for v in norms] + [dw, col(a["cv_b_dw"][0]), col(a["cv_ln_g"][0]),
                                                     col(a["cv_ln_b"][0]), col(a["gla_b_a"][0]),
                                                     col(a["gla_norm_g"][0])], axis=1)
    bpw1 = a["cv_b_pw1"][0].reshape(2, CV_CHUNKS, 256).transpose(1, 0, 2).reshape(-1)
    rows = np.concatenate([bpw1, a["cv_b_pw2"][0], a["gla_b_r"][0], a["g_final"]])
    arrays = {
        "stream": stream, "x": a["x"], "chan": chan, "rows": rows,
        "a1": a["gla_w_a1"][0].reshape(KT, P, 16).transpose(1, 0, 2).reshape(P, KT * 16),
        "a2": a["gla_w_a2"][0], "masks": level_masks(), "ident": np.eye(P, dtype=np.float32),
    }
    arrays = {f"in_{k}_dram": np.ascontiguousarray(v) for k, v in arrays.items()}
    nc = _bacc.Bacc("TRN2", target_bir_lowering=False, num_devices=1)
    args = [nc.dram_tensor(f"in_{k}_dram", arrays[f"in_{k}_dram"].shape, mybir.dt.float32, kind="ExternalInput").ap()
            for k in INS]
    out = nc.dram_tensor("out_0_dram", (1, SEQ, D), mybir.dt.float32, kind="ExternalOutput").ap()
    build(nc, *args, out)
    r = _run(nc, [arrays], core_ids=[0])
    return r.results[0]["out_0_dram"]
```
